# Optimizing a Trainium2 kernel written in Bass

```python
import math
import jax, jax.numpy as jnp
from jax import lax
import numpy as np

D_MODEL = 1024
BATCH = 1
SEQ = 512
DEPTH = 1

CHUNK = 64
N_META = 16
Q_BLOCK = 128
ROPE_THETA = 10000.0
EPS = 1e-6
NEG_INF = -1e30
BIG_ID = 2 ** 30

DIFF_HEADS = 4
DIFF_HEAD_DIM = 64
DIFF_V_DIM = 2 * DIFF_HEAD_DIM
DIFF_QK_WIDTH = DIFF_HEADS * 2 * DIFF_HEAD_DIM
DIFF_WIDTH = DIFF_HEADS * DIFF_V_DIM

FOX_HEADS = 8
FOX_HEAD_DIM = 64
FOX_WIDTH = FOX_HEADS * FOX_HEAD_DIM

DQ_OFF = 0
DK_OFF = DQ_OFF + DIFF_QK_WIDTH
DV_OFF = DK_OFF + DIFF_QK_WIDTH
FQ_OFF = DV_OFF + DIFF_WIDTH
FK_OFF = FQ_OFF + FOX_WIDTH
FV_OFF = FK_OFF + FOX_WIDTH
FF_OFF = FV_OFF + FOX_WIDTH
GA_OFF = FF_OFF + FOX_HEADS
GB_OFF = GA_OFF + D_MODEL
IN_COLS = GB_OFF + D_MODEL

PEER_HEADS = 8
PEER_N_KEYS = 128
PEER_N_EXPERTS = PEER_N_KEYS * PEER_N_KEYS
PEER_KEY_DIM = 256
PEER_HALF = PEER_KEY_DIM // 2
PEER_TOPK = 16
PEER_TOKEN_BLOCK = 256

kernel_name = "hybrid_diff_fox_peer_block"

def _rmsnorm(x, g):
    xf = x.astype(jnp.float32)
    y = xf * lax.rsqrt(jnp.mean(xf * xf, axis=-1, keepdims=True) + EPS)
    return (y * g.astype(jnp.float32)).astype(x.dtype)

def _rope(x, T):
    d = x.shape[-1]
    inv_freq = ROPE_THETA ** (-jnp.arange(0, d, 2, dtype=jnp.float32) / d)
    ang = jnp.arange(T, dtype=jnp.float32)[:, None] * inv_freq[None, :]
    cos = jnp.concatenate([jnp.cos(ang), jnp.cos(ang)], axis=-1)
    sin = jnp.concatenate([jnp.sin(ang), jnp.sin(ang)], axis=-1)
    xf = x.astype(jnp.float32)
    x1, x2 = xf[..., : d // 2], xf[..., d // 2:]
    rot = jnp.concatenate([-x2, x1], axis=-1)
    return (xf * cos + rot * sin).astype(x.dtype)

def _blocked_attention(q, k, v, q_ids, k_ids, log_decay=None):
    B, G, H, T, d = q.shape
    dv = v.shape[-1]
    n_blk = T // Q_BLOCK
    scale = d ** -0.5

    def one_block(i):
        start = i * Q_BLOCK
        qb = lax.dynamic_slice_in_dim(q, start, Q_BLOCK, axis=3)
        s = jnp.einsum("bghqd,bghkd->bghqk", qb, k).astype(jnp.float32) * scale
        if log_decay is not None:
            cq = lax.dynamic_slice_in_dim(log_decay, start, Q_BLOCK, axis=2)
            s = s + (cq[:, None, :, :, None] - log_decay[:, None, :, None, :])
        qi = lax.dynamic_slice_in_dim(q_ids, start, Q_BLOCK, axis=0)
        allowed = k_ids[None, :] <= qi[:, None]
        s = jnp.where(allowed, s, NEG_INF)
        p = jax.nn.softmax(s, axis=-1).astype(v.dtype)
        return jnp.einsum("bghqk,bhkv->bghqv", p, v)

    out = lax.map(one_block, jnp.arange(n_blk))
    out = jnp.transpose(out, (1, 2, 3, 0, 4, 5))
    return out.reshape(B, G, H, T, dv)

def _token_mixer(h, layer, w_in, b_gate, b_forget, diff_qnorm_g, diff_knorm_g,
                 diff_lambda, diff_subln_g, fox_qnorm_g, fox_knorm_g,
                 w_branch_diff, w_branch_fox, w_out, chunk_ids, frame_ids):
    B, T, _ = h.shape
    proj = h @ w_in

    dq = proj[..., DQ_OFF:DK_OFF].reshape(B, T, 2, DIFF_HEADS, DIFF_HEAD_DIM)
    dk = proj[..., DK_OFF:DV_OFF].reshape(B, T, 2, DIFF_HEADS, DIFF_HEAD_DIM)
    dv = proj[..., DV_OFF:FQ_OFF].reshape(B, T, DIFF_HEADS, DIFF_V_DIM)
    dq = _rope(_rmsnorm(jnp.transpose(dq, (0, 2, 3, 1, 4)), diff_qnorm_g), T)
    dk = _rope(_rmsnorm(jnp.transpose(dk, (0, 2, 3, 1, 4)), diff_knorm_g), T)
    dv = jnp.transpose(dv, (0, 2, 1, 3))
    o = _blocked_attention(dq, dk, dv, chunk_ids, chunk_ids)
    lam_init = 0.8 - 0.6 * math.exp(-0.3 * layer)
    lam = diff_lambda.astype(jnp.float32)
    lam = (jnp.exp(jnp.sum(lam[0] * lam[1])) - jnp.exp(jnp.sum(lam[2] * lam[3]))
           + lam_init).astype(o.dtype)
    od = o[:, 0] - lam * o[:, 1]
    od = _rmsnorm(od, diff_subln_g) * (1.0 - lam_init)
    y_a = jnp.transpose(od, (0, 2, 1, 3)).reshape(B, T, DIFF_WIDTH)

    fq = proj[..., FQ_OFF:FK_OFF].reshape(B, T, FOX_HEADS, FOX_HEAD_DIM)
    fk = proj[..., FK_OFF:FV_OFF].reshape(B, T, FOX_HEADS, FOX_HEAD_DIM)
    fv = proj[..., FV_OFF:FF_OFF].reshape(B, T, FOX_HEADS, FOX_HEAD_DIM)
    fq = _rmsnorm(jnp.transpose(fq, (0, 2, 1, 3)), fox_qnorm_g)[:, None]
    fk = _rmsnorm(jnp.transpose(fk, (0, 2, 1, 3)), fox_knorm_g)[:, None]
    fv = jnp.transpose(fv, (0, 2, 1, 3))
    f_logit = (proj[..., FF_OFF:GA_OFF] + b_forget).astype(jnp.float32)
    log_f = jax.nn.log_sigmoid(f_logit)
    cum = jnp.transpose(jnp.cumsum(log_f, axis=1), (0, 2, 1))
    of = _blocked_attention(fq, fk, fv, frame_ids, frame_ids, log_decay=cum)[:, 0]
    y_b = jnp.transpose(of, (0, 2, 1, 3)).reshape(B, T, FOX_WIDTH)

    g_a = jax.nn.sigmoid(proj[..., GA_OFF:GB_OFF] + b_gate[:D_MODEL])
    g_b = jax.nn.sigmoid(proj[..., GB_OFF:IN_COLS] + b_gate[D_MODEL:])
    merged = g_a * (y_a @ w_branch_diff) + g_b * (y_b @ w_branch_fox)
    return merged @ w_out

def _peer(h, w_q, subkeys, u, v):
    B, T, D = h.shape
    n_tok = B * T
    n_pad = -(-n_tok // PEER_TOKEN_BLOCK) * PEER_TOKEN_BLOCK
    flat = jnp.pad(h.reshape(n_tok, D), ((0, n_pad - n_tok), (0, 0)))
    blocks = flat.reshape(n_pad // PEER_TOKEN_BLOCK, PEER_TOKEN_BLOCK, D)
    BLK = PEER_TOKEN_BLOCK

    def one_block(xb):
        q = (xb @ w_q).reshape(BLK, PEER_HEADS, 2, PEER_HALF)
        s = jnp.einsum("nhcd,hckd->nhck", q, subkeys).astype(jnp.float32)
        s1, i1 = lax.top_k(s[:, :, 0], PEER_TOPK)
        s2, i2 = lax.top_k(s[:, :, 1], PEER_TOPK)
        cand = (s1[..., :, None] + s2[..., None, :]).reshape(BLK, PEER_HEADS, PEER_TOPK * PEER_TOPK)
        cidx = (i1[..., :, None] * PEER_N_KEYS + i2[..., None, :]).reshape(BLK, PEER_HEADS, PEER_TOPK * PEER_TOPK)
        best, pos = lax.top_k(cand, PEER_TOPK)
        eidx = jnp.take_along_axis(cidx, pos, axis=-1).reshape(BLK, PEER_HEADS * PEER_TOPK)
        gate = jax.nn.softmax(best, axis=-1).reshape(BLK, PEER_HEADS * PEER_TOPK)
        ue = jnp.take(u, eidx, axis=0)
        act = jax.nn.gelu(jnp.einsum("nd,ned->ne", xb, ue), approximate=False)
        ve = jnp.take(v, eidx, axis=0)
        w = gate.astype(xb.dtype) * act
        return jnp.einsum("ne,ned->nd", w, ve)

    y = lax.map(one_block, blocks).reshape(n_pad, D)[:n_tok]
    return y.reshape(B, T, D)

def setup_inputs(seed: int = 0) -> dict:
    key = jax.random.key(seed)
    ks = jax.random.split(key, 20)
    f32 = jnp.float32
    nrm = lambda k, shape, s: jax.random.normal(k, shape, f32) * s
    gain = lambda k, shape: 1.0 + 0.05 * jax.random.normal(k, shape, f32)
    return {
        "x": jax.random.normal(ks[0], (BATCH, SEQ, D_MODEL), f32),
        "meta_tokens": nrm(ks[1], (N_META, D_MODEL), 1.0),
        "norm_mix_g": gain(ks[2], (DEPTH, D_MODEL)),
        "w_in": nrm(ks[3], (DEPTH, D_MODEL, IN_COLS), D_MODEL ** -0.5),
        "b_gate": nrm(ks[4], (DEPTH, 2 * D_MODEL), 0.02),
        "b_forget": 3.0 + nrm(ks[5], (DEPTH, FOX_HEADS), 0.1),
        "diff_qnorm_g": gain(ks[6], (DEPTH, DIFF_HEAD_DIM)),
        "diff_knorm_g": gain(ks[7], (DEPTH, DIFF_HEAD_DIM)),
        "diff_lambda": nrm(ks[8], (DEPTH, 4, DIFF_HEAD_DIM), 0.1),
        "diff_subln_g": gain(ks[9], (DEPTH, DIFF_V_DIM)),
        "fox_qnorm_g": gain(ks[10], (DEPTH, FOX_HEAD_DIM)),
        "fox_knorm_g": gain(ks[11], (DEPTH, FOX_HEAD_DIM)),
        "w_branch_diff": nrm(ks[12], (DEPTH, DIFF_WIDTH, D_MODEL), DIFF_WIDTH ** -0.5),
        "w_branch_fox": nrm(ks[13], (DEPTH, FOX_WIDTH, D_MODEL), FOX_WIDTH ** -0.5),
        "w_out": nrm(ks[14], (DEPTH, D_MODEL, D_MODEL), D_MODEL ** -0.5),
        "norm_ffn_g": gain(ks[15], (DEPTH, D_MODEL)),
        "peer_w_q": nrm(ks[16], (DEPTH, D_MODEL, PEER_HEADS * PEER_KEY_DIM), D_MODEL ** -0.5),
        "peer_subkeys": nrm(ks[17], (DEPTH, PEER_HEADS, 2, PEER_N_KEYS, PEER_HALF), PEER_HALF ** -0.5),
        "peer_u": nrm(ks[18], (DEPTH, PEER_N_EXPERTS, D_MODEL), D_MODEL ** -0.5),
        "peer_v": nrm(ks[19], (DEPTH, PEER_N_EXPERTS, D_MODEL), 0.5),
    }

def reference(x, meta_tokens, norm_mix_g, w_in, b_gate, b_forget, diff_qnorm_g,
              diff_knorm_g, diff_lambda, diff_subln_g, fox_qnorm_g, fox_knorm_g,
              w_branch_diff, w_branch_fox, w_out, norm_ffn_g, peer_w_q,
              peer_subkeys, peer_u, peer_v):
    B, S, D = x.shape
    T_ext = S + N_META
    T_pad = -(-T_ext // Q_BLOCK) * Q_BLOCK

    meta = jnp.broadcast_to(meta_tokens.astype(x.dtype)[None], (B, N_META, D))
    hstream = jnp.concatenate([meta, x], axis=1)

    pos = jnp.arange(T_pad, dtype=jnp.int32)
    chunk_ids = jnp.where(pos < N_META, 0, 1 + (pos - N_META) // CHUNK)
    chunk_ids = jnp.where(pos < T_ext, chunk_ids, BIG_ID).astype(jnp.int32)
    frame_ids = pos

    for layer in range(DEPTH):
        h = _rmsnorm(hstream, norm_mix_g[layer])
        h = jnp.pad(h, ((0, 0), (0, T_pad - T_ext), (0, 0)))
        mix = _token_mixer(h, layer, w_in[layer], b_gate[layer], b_forget[layer],
                           diff_qnorm_g[layer], diff_knorm_g[layer], diff_lambda[layer],
                           diff_subln_g[layer], fox_qnorm_g[layer], fox_knorm_g[layer],
                           w_branch_diff[layer], w_branch_fox[layer], w_out[layer],
                           chunk_ids, frame_ids)
        hstream = hstream + mix[:, :T_ext]
        h2 = _rmsnorm(hstream, norm_ffn_g[layer])
        hstream = hstream + _peer(h2, peer_w_q[layer], peer_subkeys[layer],
                                  peer_u[layer], peer_v[layer])

    return hstream[:, N_META:]


_drawn_inputs = setup_inputs


def setup_inputs(seed=0):
    import zlib

    import numpy as np

    out = dict(_drawn_inputs(seed))
    spreads = {}
    factors = {'b_gate': 3.981, 'fox_qnorm_g': 2.925, 'fox_knorm_g': 2.909}
    for name, (base, spread) in spreads.items():
        noise = np.random.default_rng([zlib.crc32(name.encode()), seed]).standard_normal(out[name].shape)
        drawn = base * np.exp(spread * noise) if base else spread * noise
        out[name] = __import__('jax').numpy.asarray(drawn.astype(out[name].dtype))
    for name, factor in factors.items():
        out[name] = (out[name] * factor).astype(out[name].dtype)
    return out
```

```python
from contextlib import ExitStack

import concourse.bass as bass
from concourse import mybir

ALU = mybir.AluOpType
ACT = mybir.ActivationFunctionType
AX = mybir.AxisListType
F32 = mybir.dt.float32
BF16 = mybir.dt.bfloat16
U32 = mybir.dt.uint32

P = 128
D = 1024
KD = D // P
SEQ = 512
N_META = 16
NT = SEQ // P
KEYS = SEQ + N_META
CHUNK = 64
EPS = 1e-6
LAMBDA_INIT = 0.2
ROPE_THETA = 10000.0

DH, DV, DPAIRS = 64, 128, 4
N_DIFF, N_FOX = 4, 8
W = 512
DQ, DK, DVO, FQ, FK, FV = (i * W for i in range(6))
FF = 6 * W
GATES = FF + N_FOX

PH, NKEYS, TOPK = 8, 128, 16
NE = PH * TOPK
RING = 8
WSLOTS = 4
WK = 2
NDIAG = 4
LOWEST = -3.0e38
MASKED = -1.0e30
MASK_W = SEQ + SEQ - P

C_ID, C_TRI, C_MASKD, C_MASKF = 0, P, 2 * P, 2 * P + MASK_W
C_W = 2 * P + 2 * MASK_W
K_MIXG, K_FQG, K_FKG, K_SUB, K_ROW0, K_ROW1, K_LSEL, K_LNEG = 0, 8, 9, 10, 11, 12, 13, 21
K_W = 29
R_FFNG, R_QG, R_KG, R_LAM, R_W = 0, D, D + 64, D + 128, D + 128 + 256


def build(nc, x, meta, w_in, b_gate, b_forget, w_bd, w_bf, w_out, w_pq, subkeys_t, experts,
          table, cols, rows, rope, out):
    with ExitStack() as ctx:
        def sb(name, shape, dt=F32):
            return ctx.enter_context(nc.sbuf_tensor(name, shape, dt))

        def sem(name):
            return ctx.enter_context(nc.semaphore(name))

        ring = sb("ring", [P, RING, 2 * D])
        hT = sb("hT", [P, KD, KEYS])
        kT = sb("kT", [P, 2, DPAIRS, KEYS])
        V = sb("V", [P, 2, NT + 1, W])
        wring = sb("wring", [P, WSLOTS, WK, W])
        hs = sb("hs", [P, 2, D])
        h2 = sb("h2", [P, 2, D])
        work = sb("work", [P, 6144])
        subk = sb("subk", [P, 2 * PH, NKEYS])
        ffng = sb("ffng", [P, D])
        ropeC = sb("ropeC", [P, 2, NT + 1, DH])
        ropeS = sb("ropeS", [P, 2, NT + 1, DH])
        ident = sb("ident", [P, 2 * P])
        ident_bf = sb("ident_bf", [P, P], BF16)
        mask_bf = sb("mask_bf", [P, 2, MASK_W], BF16)
        small = sb("small", [P, K_W])
        ones = sb("ones", [P, P])
        bgate = sb("bgate", [P, W])
        wf = sb("wf", [P, KD, N_FOX])
        bf = sb("bf", [1, N_FOX])
        logf = sb("logf", [P, NT + 1, N_FOX])
        cum2 = sb("cum2", [P, NT + 1, 2 * N_FOX])
        decR = sb("decR", [16, KEYS])
        cumT = sb("cumT", [16, SEQ])
        lamt = sb("lamt", [P, 8])
        ss = sb("ss", [P, 8])
        std = sb("std", [P, 8])
        rstd = sb("rstd", [P, 8])
        nmax = sb("nmax", [P, 16])
        psum_p = sb("psum_p", [P, 16])
        rsum = sb("rsum", [P, 16])
        iota16 = sb("iota16", [P, TOPK])
        gsum = sb("gsum", [P, 2, PH])
        idx = sb("idx", [P, 2, NE], U32)
        gate = sb("gate", [P, 2, NE])
        dots = sb("dots", [P, 2 * RING])
        acts = sb("acts", [P, 2 * RING])
        wexp = sb("wexp", [P, 2 * RING])
        diag = sb("diag", [P, NDIAG, P])

        xn = [work[:, 0:D], work[:, D:2 * D]]
        heads = work[:, 0:W]
        hA, hB, hC = work[:, W:2 * W], work[:, 2 * W:3 * W], work[:, 3 * W:4 * W]
        qT = [work[:, 512:1024].rearrange("p (j q) -> p j q", j=DPAIRS),
              work[:, 1024:1536].rearrange("p (j q) -> p j q", j=DPAIRS)]
        qraw = work[:, 1536:2048]
        qA = work[:, 2048:2560]
        probs = [work[:, 1536 + i * KEYS:1536 + (i + 1) * KEYS] for i in range(4)]
        PT = [work[:, 3648 + i * 640:3648 + (i + 1) * 640] for i in range(2)]
        ya, yb = work[:, 5120:5632], work[:, 5632:6144]
        ysq = work[:, 0:W]
        tg = work[:, 0:2048].rearrange("p (n w) -> p n w", n=4)
        merged = work[:, 2048:3072]
        mT = work[:, 3072:4096].rearrange("p (k q) -> p k q", k=KD)
        yT = work[:, 4096:5120].rearrange("p (b k q) -> p b k q", b=2, k=4)
        hsq = work[:, 5120:6144]
        h2T = work[:, 0:1024].rearrange("p (k q) -> p k q", k=KD)
        pq = work[:, 1024:2048].rearrange("p (b w) -> p b w", b=2)
        pqT = work[:, 2048:2560].rearrange("p (j q) -> p j q", j=4)
        scrap = work[:, 2560:2816]
        cand = work[:, 2816:3072]
        hot = work[:, 3072:5120].rearrange("p (h k a) -> p h k a", h=PH, k=TOPK)

        decL = [work[0:16, 0:W].rearrange("p (h q) -> p h q", h=4),
                work[0:16, 5632:5632 + W].rearrange("p (h q) -> p h q", h=4)]

        def routing(at, dt, *dims):
            n = 1
            for d in dims:
                n *= d
            v = work[:, at:at + n] if dt is F32 else work[:, at:at + n].bitcast(dt)
            names = "abc"[:len(dims)]
            return v.rearrange(f"p ({' '.join(names)}) -> p {' '.join(names)}", **dict(zip(names, dims)))

        top = routing(5120, F32, 2 * PH, TOPK)
        topi = routing(5376, U32, 2 * PH, TOPK)
        topf = routing(5632, F32, 2 * PH, TOPK)
        best = routing(5888, F32, PH, TOPK)
        posn = routing(6016, U32, PH, TOPK)
        posa = routing(0, U32, 2, PH, TOPK)
        posf = routing(256, F32, 2, PH, TOPK)
        sel = routing(512, F32, 2, PH, TOPK)

        SC = ctx.enter_context(nc.psum_tensor("SC", [P, 4 * W], F32))
        TR = ctx.enter_context(nc.psum_tensor("TR", [P, W], F32))
        OV = ctx.enter_context(nc.psum_tensor("OV", [P, W], F32))
        Y = ctx.enter_context(nc.psum_tensor("Y", [P, D], F32))

        def bank(i):
            return SC[:, i * W:(i + 1) * W]

        def meta_T(c):
            b = (c % 2) * 2 * W
            return SC[0:N_META, b + 640:b + 640 + P]

        consts_in = sem("consts_in")
        x_in = [sem("x_in0"), sem("x_in1")]
        w_in_sem = [sem(f"w_landed{i}") for i in range(WSLOTS)]
        chunk_done = sem("chunk_done")
        dve_step = sem("dve_step")
        act_step = sem("act_step")
        setup = sem("setup")
        iota_ready = sem("iota_ready")
        sq_ready = sem("sq_ready")
        var_ready = sem("var_ready")
        std_ready = sem("std_ready")
        xn_ready = sem("xn_ready")
        xT_ready = sem("xT_ready")
        hT_ready = sem("hT_ready")
        kv_ready = sem("kv_ready")
        heads_ready = sem("heads_ready")
        headsT_ready = sem("headsT_ready")
        qk_ready = sem("qk_ready")
        v_copied = sem("v_copied")
        f_ready = sem("f_ready")
        f_neg = sem("f_neg")
        f_soft = sem("f_soft")
        logf_ready = sem("logf_ready")
        cum_ready = sem("cum_ready")
        cum_copied = sem("cum_copied")
        cumT_ready = sem("cumT_ready")
        dec_ready = sem("dec_ready")
        lam_dots = sem("lam_dots")
        lam_exp = sem("lam_exp")
        scores_ready = sem("scores_ready")
        max_ready = sem("max_ready")
        exp_ready = sem("exp_ready")
        mix_ready = sem("mix_ready")
        PT_ready = sem("PT_ready")
        PT_copied = sem("PT_copied")
        PTm_copied = sem("PTm_copied")
        pv_done = sem("pv_done")
        od_copied = sem("od_copied")
        yb_ready = sem("yb_ready")
        ya_ready = sem("ya_ready")
        yT_psum = sem("yT_psum")
        yT_ready = sem("yT_ready")
        tanh_ready = sem("tanh_ready")
        merged_ready = sem("merged_ready")
        mT_psum = sem("mT_psum")
        mT_ready = sem("mT_ready")
        hs_ready = sem("hs_ready")
        h2_ready = sem("h2_ready")
        h2T_psum = sem("h2T_psum")
        h2T_ready = sem("h2T_ready")
        pq_copied = sem("pq_copied")
        pqT_psum = sem("pqT_psum")
        pqT_copied = sem("pqT_copied")
        key_scores = sem("key_scores")
        keys_taken = sem("keys_taken")
        gate_shift = sem("gate_shift")
        gate_exp = sem("gate_exp")
        route_ready = sem("route_ready")
        row_landed = [sem(f"row_landed{i}") for i in range(RING)]
        dot_ready = sem("dot_ready")
        act_ready = sem("act_ready")
        wexp_ready = sem("wexp_ready")
        diag_ready = sem("diag_ready")
        rochunk_done = sem("rochunk_done")
        out_ready = sem("out_ready")
        out_stored = sem("out_stored")

        N_CONST = 10
        KV = [DK, FK, DVO, FV]
        tiles = [(s * P, P) for s in range(NT)] + [(SEQ, N_META)]
        NKT = len(tiles)

        def chunks(w, c0, k_tiles):
            v = w.rearrange("(k p) n -> p k n", p=P)
            return [v[:, k:k + WK, c0:c0 + W] for k in range(0, k_tiles, WK)]

        first_chunks = [c for g in KV for c in chunks(w_in, g, KD)]
        tile_chunks = ([c for g in (DQ, FQ) for c in chunks(w_in, g, KD)]
                       + [c for n in range(4) for c in chunks(w_in, GATES + n * W, KD)]
                       + [c for w in (w_bd, w_bf) for n in range(2) for c in chunks(w, n * W, 4)]
                       + [c for n in range(2) for c in chunks(w_out, n * W, KD)]
                       + [c for n in range(4) for c in chunks(w_pq, n * W, KD)])
        NF, NW = len(first_chunks), len(tile_chunks)
        assert NF % WSLOTS == 0 and NW % WSLOTS == 0
        CH_Q, CH_G = 0, 2 * KD // WK
        CH_B = CH_G + 4 * KD // WK
        CH_O = CH_B + 4 * 4 // WK
        CH_P = CH_O + 2 * KD // WK

        def group_done(t, first, j, k_tiles=KD):
            return NF + t * NW + first + (j + 1) * k_tiles // WK

        def wait_kv(eng, g, s):
            if s < NKT - 1:
                eng.wait_ge(kv_ready, g * (NKT - 1) + s + 1)
            else:
                eng.wait_ge(chunk_done, (g + 1) * KD // WK)

        block = ctx.enter_context(nc.Block())

        @block.sync
        def _(sp):
            def load_x(i, t):
                c0, r = tiles[t]
                src = x[c0:c0 + r, :] if t < NT else meta
                sp.dma_start(hs[0:r, i % 2, :], src).then_inc(x_in[i % 2], 16)

            load_x(0, 0)
            load_x(1, 1)
            for dst, src in ((small[:, :], cols), (ident[:, :], table[:, 0:2 * P]),
                             (work[:, 2048:2048 + 2 * MASK_W], table[:, 2 * P:C_W]),
                             (ropeC[:, 0, :, :], rope[:, :, 0:DH]), (ropeS[:, 0, :, :], rope[:, :, DH:2 * DH]),
                             (work[:, 4096:4096 + R_W - D], rows[:, D:R_W]), (ffng[:, :], rows[:, 0:D]),
                             (subk[:, :, :], subkeys_t),
                             (wf[:, :, :], w_in[:, FF:FF + N_FOX].rearrange("(k p) n -> p k n", p=P)),
                             (bf[:, :], b_forget)):
                sp.dma_start(dst, src).then_inc(consts_in, 16)
            for n in range(4):
                sp.dma_start(bgate[32 * n:32 * n + 1, :], b_gate[:, n * W:(n + 1) * W]).then_inc(consts_in, 16)
            for t in range(2, NKT):
                sp.wait_ge(xn_ready, t - 1)
                load_x(t, t)
            for n, c in enumerate(first_chunks):
                if n >= WSLOTS:
                    sp.wait_ge(chunk_done, n - WSLOTS + 1)
                sp.dma_start(wring[:, n % WSLOTS, :, :], c).then_inc(w_in_sem[n % WSLOTS], 16)
            sp.wait_ge(xn_ready, NKT)
            for t in range(NT):
                if t >= 2:
                    sp.wait_ge(out_stored, 16 * (t - 1))
                load_x(NKT + 1 + t, t)
                for n, c in enumerate(tile_chunks):
                    sp.wait_ge(chunk_done, NF + t * NW + n - WSLOTS + 1)
                    sp.dma_start(wring[:, n % WSLOTS, :, :], c).then_inc(w_in_sem[n % WSLOTS], 16)
                sp.wait_ge(out_ready, t + 1)
                sp.dma_start(out[t * P:(t + 1) * P, :], hs[:, (NKT + 1 + t) % 2, :]).then_inc(out_stored, 16)
            sp.wait_ge(out_stored, 16 * NT)

        CONSTS = 16 * (N_CONST + 4)

        def hsb(t):
            return (NKT + 1 + t) % 2

        def x_count(t):
            i = NKT + 1 + t
            return 16 * len([j for j in [*range(NKT), *range(NKT + 1, i + 1)] if j % 2 == i % 2])

        @block.tensor
        def _(pe):
            idm = ident[:, 0:P]
            tri = ident[:, P:2 * P]

            def use_chunks(n0, k_tiles, lhs, acc, bias=None):
                if bias is not None:
                    nc.tensor.matmul(acc, *bias, start=True, stop=False)
                for j in range(k_tiles // WK):
                    n = n0 + j
                    pe.wait_ge(w_in_sem[n % WSLOTS], 16 * (n // WSLOTS + 1))
                    for i in range(WK):
                        k = j * WK + i
                        mm = nc.tensor.matmul(acc, lhs(k), wring[:, n % WSLOTS, i, :],
                                              start=(k == 0 and bias is None), stop=(k == k_tiles - 1))
                    mm.then_inc(chunk_done, 1)

            pe.wait_ge(consts_in, CONSTS)
            for s, (c0, r) in enumerate(tiles):
                pe.wait_ge(xn_ready, s + 1)
                if s >= 2:
                    pe.wait_ge(hT_ready, s - 1)
                for k in range(KD):
                    mm = nc.tensor.transpose(SC[:, (s % 2) * D + k * P:(s % 2) * D + k * P + r],
                                             xn[s % 2][0:r, k * P:(k + 1) * P], ident[0:r, 0:r])
                mm.then_inc(xT_ready, 1)

            def headsT(i, r):
                pe.wait_ge(heads_ready, i + 1)
                if i >= 1:
                    pe.wait_ge(qk_ready, i)
                for j in range(DPAIRS):
                    mm = nc.tensor.transpose(TR[:, j * P:j * P + r], heads[0:r, j * P:(j + 1) * P],
                                             ident[0:r, 0:r])
                mm.then_inc(headsT_ready, 1)

            pe.wait_ge(hT_ready, NKT)
            pe.wait_ge(setup, 1)
            for g in range(4):
                for j in range(KD // WK):
                    n = g * (KD // WK) + j
                    pe.wait_ge(w_in_sem[n % WSLOTS], 16 * (n // WSLOTS + 1))
                    for s, (c0, r) in enumerate(tiles):
                        acc = bank(s) if s < 4 else OV[:, :]
                        if j == 0 and g > 0:
                            if g <= 2:
                                pe.wait_ge(heads_ready, (g - 1) * NKT + s + 1)
                            else:
                                pe.wait_ge(v_copied, s + 1)
                        for i in range(WK):
                            k = j * WK + i
                            mm = nc.tensor.matmul(acc[0:r, :], hT[:, k, c0:c0 + r],
                                                  wring[:, n % WSLOTS, i, :], start=(k == 0), stop=(k == KD - 1))
                        if s < NKT - 1 and j == KD // WK - 1:
                            mm.then_inc(kv_ready, 1)
                        if s == NKT - 1:
                            mm.then_inc(chunk_done, 1)
                if g < 2:
                    for s, (c0, r) in enumerate(tiles):
                        headsT(g * NKT + s, r)

            pe.wait_ge(qk_ready, 2 * NKT)
            for s, (c0, r) in enumerate(tiles):
                o = TR[0:r, s * N_FOX:(s + 1) * N_FOX]
                for k in range(KD):
                    nc.tensor.matmul(o, hT[:, k, c0:c0 + r], wf[:, k, :], start=(k == 0), stop=False)
                mm = nc.tensor.matmul(o, ones[0:1, 0:r], bf[:, :], start=False, stop=True)
            mm.then_inc(f_ready, 1)
            pe.wait_ge(logf_ready, 1)
            for s, (c0, r) in enumerate(tiles):
                o = Y[0:r, s * N_FOX:(s + 1) * N_FOX]
                if s < NT:
                    nc.tensor.matmul(o, ones[0:N_META, :], logf[0:N_META, NT, :], start=True, stop=False)
                    for b in range(s):
                        nc.tensor.matmul(o, ones[:, :], logf[:, b, :], start=False, stop=False)
                    mm = nc.tensor.matmul(o, tri, logf[:, s, :], start=False, stop=True)
                else:
                    mm = nc.tensor.matmul(o, tri[0:N_META, 0:N_META], logf[0:N_META, NT, :],
                                          start=True, stop=True)
            mm.then_inc(cum_ready, 1)
            pe.wait_ge(cum_copied, 1)
            for s, (c0, r) in enumerate(tiles):
                mm = nc.tensor.transpose(Y[0:16, c0:c0 + r], cum2[0:r, s, :], ident[0:r, 0:r])
            mm.then_inc(cumT_ready, 1)

            def unit(c):
                return c // 2 if c < 2 * N_DIFF else c - N_DIFF

            def scores(t, c):
                n = 16 * t + c
                if c >= 2:
                    pe.wait_ge(exp_ready, n - 1)
                if c >= 10 or c == 9 or (c % 2 == 1 and c >= 3):
                    pe.wait_ge(PTm_copied, 12 * t + (c - 5 if c >= 9 else (c - 1) // 2))
                fox = c >= 2 * N_DIFF
                g = c - 8 if fox else (c % 2) * N_DIFF + c // 2
                lo = DH * (g % 2)
                q = qT[fox][lo:lo + DH, g // 2, :]
                b = (c % 2) * 2 * W
                acc, accm = SC[:, b:b + SEQ], SC[:, b + SEQ:b + KEYS]
                w0 = SEQ - P - t * P
                nc.tensor.matmul(acc, ident_bf[:, :], mask_bf[:, int(fox), w0:w0 + SEQ], start=True, stop=False)
                nc.tensor.matmul(acc, q, kT[lo:lo + DH, int(fox), g // 2, 0:SEQ], start=False, stop=not fox)
                if fox:
                    nc.tensor.matmul(acc, decL[g // 4][:, g % 4, :], decR[:, 0:SEQ], start=False, stop=True)
                mm = nc.tensor.matmul(accm, q, kT[lo:lo + DH, int(fox), g // 2, SEQ:KEYS], start=True, stop=not fox)
                if fox:
                    mm = nc.tensor.matmul(accm, decL[g // 4][:, g % 4, :], decR[:, SEQ:KEYS], start=False, stop=True)
                mm.then_inc(scores_ready, 1)

            def unit_scores(t, u):
                for c in ((2 * u, 2 * u + 1) if u < N_DIFF else (u + N_DIFF,)):
                    scores(t, c)

            def probsT(t, u):
                c = 2 * u + 1 if u < N_DIFF else u + N_DIFF
                if u < N_DIFF:
                    pe.wait_ge(mix_ready, N_DIFF * t + u + 1)
                else:
                    pe.wait_ge(exp_ready, 16 * t + c + 1)
                if u >= 1:
                    pe.wait_ge(PT_copied, 12 * t + u)
                    pe.wait_ge(PTm_copied, 12 * t + u)
                pr = probs[c % 4]
                for s in range(NT):
                    nc.tensor.transpose(TR[:, s * P:(s + 1) * P], pr[:, s * P:(s + 1) * P], idm)
                nc.tensor.transpose(meta_T(c), pr[:, SEQ:KEYS], idm).then_inc(PT_ready, 1)

            def pv(t, u):
                n = 12 * t + u
                pe.wait_ge(PT_copied, n + 1)
                pe.wait_ge(PTm_copied, n + 1)
                if u == N_DIFF:
                    pe.wait_ge(od_copied, t + 1)
                fox = u >= N_DIFF
                wv = DH if fox else DV
                h = u - N_DIFF if fox else u
                o = OV[:, h * wv:(h + 1) * wv]
                pt = PT[u % 2]
                for s in range(NT):
                    nc.tensor.matmul(o, pt[:, s * P:(s + 1) * P], V[:, int(fox), s, h * wv:(h + 1) * wv],
                                     start=(s == 0), stop=False)
                nc.tensor.matmul(o, pt[0:N_META, SEQ:SEQ + P], V[0:N_META, int(fox), NT, h * wv:(h + 1) * wv],
                                 start=False, stop=True).then_inc(pv_done, 1)

            for t in range(NT):
                n0 = NF + t * NW
                if t == 0:
                    pe.wait_ge(v_copied, 2 * NKT)
                    pe.wait_ge(dec_ready, 1)
                else:
                    pe.wait_ge(pq_copied, 4 * t)
                for g in range(2):
                    use_chunks(n0 + CH_Q + g * KD // WK, KD, lambda k: hT[:, k, t * P:(t + 1) * P], bank(g))
                for g in range(2):
                    headsT(2 * NKT + 2 * t + g, P)
                pe.wait_ge(qk_ready, 2 * NKT + 2 * t + 2)
                pe.wait_ge(dec_ready, t + 2)
                if t >= 1:
                    pe.wait_ge(keys_taken, 4 * t)
                for u in range(N_DIFF):
                    unit_scores(t, u)
                    if u >= 1:
                        pv(t, u - 1)
                    probsT(t, u)
                unit_scores(t, N_DIFF)
                pv(t, N_DIFF - 1)
                for u in range(N_DIFF, 12):
                    if u + 1 < 12:
                        unit_scores(t, u + 1)
                    probsT(t, u)
                    if u > N_DIFF:
                        pv(t, u - 1)
                pv(t, 11)
                for n in range(4):
                    if n == 0:
                        pe.wait_ge(exp_ready, 16 * (t + 1))
                    use_chunks(n0 + CH_G + n * KD // WK, KD, lambda k: hT[:, k, t * P:(t + 1) * P], bank(n),
                               (ones[32 * n:32 * n + 1, :], bgate[32 * n:32 * n + 1, :]))
                for b in range(2):
                    if b == 0:
                        pe.wait_ge(ya_ready, t + 1)
                    else:
                        pe.wait_ge(yb_ready, t + 1)
                        pe.wait_ge(yT_ready, 2 * t + 1)
                    for j in range(4):
                        mm = nc.tensor.transpose(TR[:, j * P:(j + 1) * P], (ya, yb)[b][:, j * P:(j + 1) * P], idm)
                    mm.then_inc(yT_psum, 1)
                for b in range(2):
                    pe.wait_ge(yT_ready, 2 * t + b + 1)
                    for n in range(2):
                        pe.wait_ge(tanh_ready, 4 * t + 2 * b + n + 1)
                        use_chunks(n0 + CH_B + (2 * b + n) * 4 // WK, 4, lambda k: yT[:, b, k, :],
                                   bank(2 * b + n))
                pe.wait_ge(merged_ready, 2 * t + 2)
                for k in range(KD):
                    mm = nc.tensor.transpose(SC[:, k * P:(k + 1) * P], merged[:, k * P:(k + 1) * P], idm)
                mm.then_inc(mT_psum, 1)
                pe.wait_ge(mT_ready, t + 1)
                for n in range(2):
                    use_chunks(n0 + CH_O + n * KD // WK, KD, lambda k: mT[:, k, :], bank(2 + n))
                pe.wait_ge(h2_ready, t + 1)
                for k in range(KD):
                    mm = nc.tensor.transpose(SC[:, k * P:(k + 1) * P], h2[:, hsb(t), k * P:(k + 1) * P], idm)
                mm.then_inc(h2T_psum, 1)
                pe.wait_ge(h2T_ready, t + 1)
                for n in range(4):
                    m = 4 * t + n
                    if n >= 2:
                        pe.wait_ge(pq_copied, m - 1)
                    use_chunks(n0 + CH_P + n * KD // WK, KD, lambda k: h2T[:, k, :],
                               bank(2 + n % 2))
                    pe.wait_ge(pq_copied, m + 1)
                    if n >= 1:
                        pe.wait_ge(pqT_copied, m)
                    for j in range(4):
                        mm = nc.tensor.transpose(TR[:, j * P:(j + 1) * P], pq[:, n % 2, j * P:(j + 1) * P], idm)
                    mm.then_inc(pqT_psum, 1)
                    pe.wait_ge(pqT_copied, m + 1)
                    if m >= 1:
                        pe.wait_ge(keys_taken, m)
                    for j in range(4):
                        mm = nc.tensor.matmul(OV[:, j * P:(j + 1) * P], pqT[:, j, :], subk[:, 4 * n + j, :],
                                              start=True, stop=True)
                    mm.then_inc(key_scores, 1)
                for e in range(NE):
                    n = NE * t + e
                    pe.wait_ge(diag_ready, n + 1)
                    for i in range(2):
                        mm = nc.tensor.matmul(Y[:, i * W:(i + 1) * W], diag[:, e % NDIAG, :],
                                              ring[:, e % RING, D + i * W:D + (i + 1) * W],
                                              start=(e == 0), stop=(e == NE - 1))
                    mm.then_inc(rochunk_done, 1)
                if t < NT - 1:
                    pe.wait_ge(out_ready, t + 1)

        @block.scalar
        def _(act):
            steps = [0]

            def after(ins):
                steps[0] += 1
                ins.then_inc(act_step, 1)
                act.wait_ge(act_step, steps[0])

            nsq, nvar = [0], [0]

            def squares(dst, src, acc=None):
                nc.scalar.activation(dst, src, ACT.Square, accum_out=acc).then_inc(sq_ready, 1)

            def root(r, n):
                nvar[0] += 1
                act.wait_ge(var_ready, nvar[0])
                nc.scalar.activation(std[0:r, 0:n], ss[0:r, 0:n], ACT.Sqrt).then_inc(std_ready, 1)

            act.wait_ge(lam_dots, 2)
            nc.scalar.activation(lamt[:, 2:4], lamt[:, 0:2], ACT.Exp).then_inc(lam_exp, 1)
            for s, (c0, r) in enumerate(tiles):
                act.wait_ge(x_in[s % 2], 16 * (s // 2 + 1))
                if s >= 1:
                    act.wait_ge(xn_ready, s)
                squares(ring[0:r, s, 0:D], hs[0:r, s % 2, :], ss[0:r, 0:1])
                root(r, 1)
            for i in range(2 * NKT):
                g, s = divmod(i, NKT)
                r = tiles[s][1]
                wait_kv(act, g, s)
                if i >= 1:
                    act.wait_ge(heads_ready, i)
                squares(hA[0:r, :], (bank(s) if s < 4 else OV)[0:r, :])
                root(r, 8)
            for i in range(2 * NKT):
                g, s = divmod(i, NKT)
                r = tiles[s][1]
                wait_kv(act, 2 + g, s)
                nc.scalar.activation(V[0:r, g, s, :], (bank(s) if s < 4 else OV)[0:r, :],
                                     ACT.Copy).then_inc(v_copied, 1)
            act.wait_ge(f_neg, 2)
            after(nc.scalar.activation(cum2[:, :, 0:8], cum2[:, :, 8:16], ACT.Exp))
            nc.scalar.activation(cum2[:, :, 0:8], cum2[:, :, 0:8], ACT.Ln, bias=1.0).then_inc(f_soft, 1)

            def copy_PT(t, u):
                n = 12 * t + u
                act.wait_ge(PT_ready, n + 1)
                if n >= 2:
                    act.wait_ge(pv_done, n - 1)
                nc.scalar.activation(PT[u % 2][:, 0:SEQ], TR[:, :], ACT.Copy).then_inc(PT_copied, 1)

            for t in range(NT):
                for g in range(2):
                    i = 2 * NKT + 2 * t + g
                    act.wait_ge(chunk_done, group_done(t, CH_Q, g))
                    act.wait_ge(heads_ready, i)
                    squares(qA[:, :], bank(g))
                    root(P, 8)

                def exps(c):
                    n = 16 * t + c
                    act.wait_ge(max_ready, n + 1)
                    if c >= 4:
                        v = c - 4
                        act.wait_ge(PT_ready, 12 * t + (v // 2 if v < 8 else v - 4) + 1)
                    b = (c % 2) * 2 * W
                    nc.scalar.activation(probs[c % 4], SC[:, b:b + KEYS], ACT.Exp, bias=nmax[:, c:c + 1],
                                         accum_out=psum_p[:, c:c + 1]).then_inc(exp_ready, 1)

                exps(0)
                exps(1)
                for u in range(12):
                    v = u + 1
                    if v < 12:
                        for c in ((2 * v, 2 * v + 1) if v < N_DIFF else (v + N_DIFF,)):
                            exps(c)
                    copy_PT(t, u)
                act.wait_ge(od_copied, t + 1)
                squares(ysq, ya)
                root(P, 4)
                act.wait_ge(ya_ready, t + 1)
                for n in range(4):
                    act.wait_ge(chunk_done, group_done(t, CH_G, n))
                    nc.scalar.activation(tg[:, n, :], bank(n), ACT.Tanh, scale=0.5).then_inc(tanh_ready, 1)
                act.wait_ge(mT_psum, t + 1)
                nc.scalar.activation(mT.rearrange("p k q -> p (k q)"), SC[:, 0:D], ACT.Copy).then_inc(mT_ready, 1)
                act.wait_ge(hs_ready, 2 * t + 2)
                squares(hsq, hs[:, hsb(t), :], ss[:, 0:1])
                root(P, 1)
                act.wait_ge(h2T_psum, t + 1)
                nc.scalar.activation(h2T.rearrange("p k q -> p (k q)"), SC[:, 0:D], ACT.Copy).then_inc(h2T_ready, 1)
                for n in range(4):
                    m = 4 * t + n
                    act.wait_ge(chunk_done, group_done(t, CH_P, n))
                    nc.scalar.activation(pq[:, n % 2, :], bank(2 + n % 2), ACT.Copy).then_inc(pq_copied, 1)
                    act.wait_ge(pqT_psum, m + 1)
                    if n >= 1:
                        act.wait_ge(key_scores, m)
                    nc.scalar.activation(pqT.rearrange("p j q -> p (j q)"), TR[:, :], ACT.Copy).then_inc(pqT_copied, 1)
                act.wait_ge(gate_shift, t + 1)
                g_ = gate[:, t % 2, :]
                nc.scalar.activation(g_, g_, ACT.Exp).then_inc(gate_exp, 1)
                for e in range(0, NE, 2):
                    act.wait_ge(dot_ready, NE * t + e + 2)
                    w = e % (2 * RING)
                    nc.scalar.activation(acts[:, w:w + 2], dots[:, w:w + 2], ACT.Gelu).then_inc(act_ready, 1)
                    act.wait_ge(wexp_ready, (NE * t + e) // 2 + 1)
                    for j in (e, e + 1):
                        n = NE * t + j
                        if n >= NDIAG:
                            act.wait_ge(rochunk_done, n - NDIAG + 1)
                        nc.scalar.activation(diag[:, j % NDIAG, :], ident[:, 0:P], ACT.Copy,
                                             scale=wexp[:, j % (2 * RING):j % (2 * RING) + 1]).then_inc(diag_ready, 1)

        @block.vector
        def _(dve):
            steps = [0]

            def after(ins):
                steps[0] += 1
                ins.then_inc(dve_step, 1)
                dve.wait_ge(dve_step, steps[0])

            nsq = [0]

            def inverse_root(r, n, width, scale=None):
                nsq[0] += 1
                nc.vector.tensor_scalar(ss[0:r, 0:n], ss[0:r, 0:n], 1.0 / width, EPS, ALU.mult,
                                        ALU.add).then_inc(var_ready, 1)
                dve.wait_ge(std_ready, nsq[0])
                after(nc.vector.reciprocal(rstd[0:r, 0:n], std[0:r, 0:n]))
                if scale is not None:
                    after(nc.vector.tensor_scalar(rstd[0:r, 0:n], rstd[0:r, 0:n], scale, None, ALU.mult))

            nc.vector.memset(ones[:, :], 1.0)
            nc.vector.memset(cum2[:, :, :], 0.0)
            after(nc.vector.memset(logf[:, :, :], 0.0))
            dve.wait_ge(consts_in, CONSTS)
            m0 = 2048
            nc.vector.tensor_copy(mask_bf[:, 0, :], work[:, m0:m0 + MASK_W])
            nc.vector.tensor_copy(mask_bf[:, 1, :], work[:, m0 + MASK_W:m0 + 2 * MASK_W])
            after(nc.vector.tensor_copy(ident_bf[:, :], ident[:, 0:P]))
            rw = work[:, 4096:4096 + R_W - D]
            qg, kg, lam = rw[:, 0:DH], rw[:, DH:2 * DH], rw[:, 2 * DH:2 * DH + 4 * DH]
            H = DH // 2
            for which, g in ((1, kg), (0, qg)):
                def gb(lo, hi):
                    return g[:, lo:hi].unsqueeze(1).to_broadcast([P, NKT, hi - lo])
                nc.vector.tensor_tensor(ropeC[:, which, :, :], ropeC[:, 0, :, :], gb(0, DH), ALU.mult)
                nc.vector.tensor_tensor(ropeS[:, which, :, 0:H], ropeS[:, 0, :, 0:H], gb(H, DH), ALU.mult)
                after(nc.vector.tensor_tensor(ropeS[:, which, :, H:DH], ropeS[:, 0, :, H:DH], gb(0, H), ALU.mult))
            for i in range(2):
                nc.vector.tensor_tensor_reduce(out=work[:, 5120:5120 + DH], in0=lam[:, 2 * i * DH:(2 * i + 1) * DH],
                                               in1=lam[:, (2 * i + 1) * DH:(2 * i + 2) * DH], scale=1.0, scalar=0.0,
                                               op0=ALU.mult, op1=ALU.add,
                                               accum_out=lamt[:, i:i + 1]).then_inc(lam_dots, 1)
                dve.wait_ge(lam_dots, i + 1)
            dve.wait_ge(lam_exp, 1)
            after(nc.vector.tensor_tensor(lamt[:, 4:5], lamt[:, 3:4], lamt[:, 2:3], ALU.subtract))
            nc.vector.tensor_scalar(lamt[:, 5:6], lamt[:, 4:5], -LAMBDA_INIT, None, ALU.add).then_inc(setup, 1)
            dve.wait_ge(setup, 1)

            def put_hT(s):
                c0, r = tiles[s]
                dve.wait_ge(xT_ready, s + 1)
                src = SC[:, (s % 2) * D:(s % 2 + 1) * D].rearrange("p (k q) -> p k q", k=KD)[:, :, 0:r]
                nc.vector.tensor_tensor(hT[:, :, c0:c0 + r], src,
                                        small[:, K_MIXG:K_MIXG + KD].unsqueeze(2).to_broadcast([P, KD, r]),
                                        ALU.mult).then_inc(hT_ready, 1)

            for s, (c0, r) in enumerate(tiles):
                dve.wait_ge(sq_ready, s + 1)
                inverse_root(r, 1, D)
                if s >= 2:
                    dve.wait_ge(xT_ready, s - 1)
                nc.vector.tensor_scalar(xn[s % 2][0:r, :], hs[0:r, s % 2, :], rstd[0:r, 0:1], None,
                                        ALU.mult).then_inc(xn_ready, 1)
                if s >= 1:
                    put_hT(s - 1)
            put_hT(NKT - 1)

            def norm_heads(i, r, psum, sqs, raw, which, tile, scale):
                dve.wait_ge(sq_ready, NKT + i + 1 + extra_sq(i))
                v3 = lambda a: a.rearrange("p (g d) -> p g d", g=8)
                after(nc.vector.tensor_reduce(ss[0:r, 0:8], v3(sqs[0:r, :]), AX.X, ALU.add))
                inverse_root(r, 8, DH, scale)
                rb = rstd[0:r, 0:8].unsqueeze(2).to_broadcast([r, 8, DH])
                if i >= 1:
                    dve.wait_ge(headsT_ready, i)
                if which is None:
                    nc.vector.tensor_tensor(v3(heads[0:r, :]), v3(psum[0:r, :]), rb, ALU.mult).then_inc(heads_ready, 1)
                    return
                after(nc.vector.tensor_tensor(v3(raw[0:r, :]), v3(psum[0:r, :]), rb, ALU.mult))
                C = ropeC[0:r, which, tile, :].unsqueeze(1).to_broadcast([r, 8, DH])
                S = ropeS[0:r, which, tile, :]
                nc.vector.tensor_tensor(v3(heads[0:r, :]), v3(raw[0:r, :]), C, ALU.mult)
                H = DH // 2
                for lo, src in ((0, H), (H, 0)):
                    ins = nc.vector.tensor_tensor(v3(sqs[0:r, :])[:, :, lo:lo + H], v3(raw[0:r, :])[:, :, src:src + H],
                                                  S[:, lo:lo + H].unsqueeze(1).to_broadcast([r, 8, H]), ALU.mult)
                after(ins)
                nc.vector.tensor_tensor(heads[0:r, :], heads[0:r, :], sqs[0:r, :], ALU.add).then_inc(heads_ready, 1)

            def extra_sq(i):
                return 0 if i < 2 * NKT else 2 * ((i - 2 * NKT) // 2)

            def put_T(i, dst, r, gain):
                dve.wait_ge(headsT_ready, i + 1)
                src = TR[:, :].rearrange("p (j q) -> p j q", j=DPAIRS)[:, :, 0:r]
                if gain is None:
                    nc.vector.tensor_copy(dst, src).then_inc(qk_ready, 1)
                else:
                    nc.vector.tensor_scalar(dst, src, gain, None, ALU.mult).then_inc(qk_ready, 1)

            for i in range(2 * NKT):
                g, s = divmod(i, NKT)
                c0, r = tiles[s]
                norm_heads(i, r, bank(s) if s < 4 else OV, hA, hB, 1 if g == 0 else None, s, None)
                put_T(i, kT[:, g, :, c0:c0 + r], r, None if g == 0 else small[:, K_FKG:K_FKG + 1])

            dve.wait_ge(f_ready, 1)
            for lo, n, r in ((0, NT, P), (NT, 1, N_META)):
                z = TR[0:r, lo * N_FOX:(lo + n) * N_FOX].rearrange("p (s h) -> p s h", s=n)
                after(nc.vector.tensor_scalar(logf[0:r, lo:lo + n, :], z, 0.0, None, ALU.min))
                after(nc.vector.tensor_scalar(cum2[0:r, lo:lo + n, 8:16], z, 0.0, None, ALU.max))
                nc.vector.tensor_tensor(cum2[0:r, lo:lo + n, 8:16], logf[0:r, lo:lo + n, :],
                                        cum2[0:r, lo:lo + n, 8:16], ALU.subtract).then_inc(f_neg, 1)
            dve.wait_ge(f_soft, 1)
            nc.vector.tensor_tensor(logf[:, :, :], logf[:, :, :], cum2[:, :, 0:8], ALU.subtract).then_inc(logf_ready, 1)
            dve.wait_ge(cum_ready, 1)
            for lo, n, r in ((0, NT, P), (NT, 1, N_META)):
                for j in range(2):
                    ins = nc.vector.tensor_copy(cum2[0:r, lo:lo + n, 8 * j:8 * j + 8],
                                                Y[0:r, lo * N_FOX:(lo + n) * N_FOX].rearrange("p (s h) -> p s h", s=n))
            ins.then_inc(cum_copied, 1)
            dve.wait_ge(cumT_ready, 1)
            nc.vector.tensor_scalar(decR[:, :], Y[0:16, 0:KEYS], small[0:16, K_ROW0:K_ROW0 + 1],
                                    small[0:16, K_ROW1:K_ROW1 + 1], ALU.mult, ALU.add)
            nc.vector.tensor_copy(cumT[:, :], Y[0:16, 0:SEQ]).then_inc(dec_ready, 1)
            dve.wait_ge(dec_ready, 1)

            for t in range(NT):
                for g in range(2):
                    i = 2 * NKT + 2 * t + g
                    norm_heads(i, P, bank(g), qA, qraw, 0 if g == 0 else None, t, DH ** -0.5)
                    put_T(i, qT[g], P, None if g == 0 else small[:, K_FQG:K_FQG + 1])
                for h in range(N_FOX):
                    ins = nc.vector.tensor_scalar(decL[h // 4][:, h % 4, :], cumT[:, t * P:(t + 1) * P],
                                                  small[0:16, K_LSEL + h:K_LSEL + h + 1],
                                                  small[0:16, K_LNEG + h:K_LNEG + h + 1], ALU.mult, ALU.add)
                ins.then_inc(dec_ready, 1)

                def row_max(c):
                    dve.wait_ge(scores_ready, 16 * t + c + 1)
                    b = (c % 2) * 2 * W
                    nc.vector.tensor_reduce(nmax[:, c:c + 1], SC[:, b:b + KEYS], AX.X, ALU.max,
                                            negate=True).then_inc(max_ready, 1)

                def unit_max(u):
                    for c in ((2 * u, 2 * u + 1) if u < N_DIFF else (u + N_DIFF,)):
                        row_max(c)

                unit_max(0)
                for u in range(12):
                    if u < N_DIFF:
                        c = 2 * u
                        dve.wait_ge(exp_ready, 16 * t + c + 2)
                        after(nc.vector.reciprocal(rsum[:, c:c + 2], psum_p[:, c:c + 2]))
                        nc.vector.tensor_scalar(probs[c % 4], probs[c % 4], rsum[:, c:c + 1], None, ALU.mult)
                        after(nc.vector.tensor_scalar(rsum[:, c + 1:c + 2], rsum[:, c + 1:c + 2], lamt[:, 5:6], None,
                                                      ALU.mult))
                        nc.vector.scalar_tensor_tensor(out=probs[c % 4 + 1], in0=probs[c % 4 + 1],
                                                       scalar=rsum[:, c + 1:c + 2], in1=probs[c % 4],
                                                       op0=ALU.mult, op1=ALU.add).then_inc(mix_ready, 1)
                    if u >= N_DIFF and u + 1 < 12:
                        unit_max(u + 1)
                    n = 12 * t + u
                    dve.wait_ge(PT_ready, n + 1)
                    if n >= 2:
                        dve.wait_ge(pv_done, n - 1)
                    nc.vector.tensor_copy(PT[u % 2][0:N_META, SEQ:SEQ + P],
                                          meta_T(2 * u + 1 if u < N_DIFF else u + N_DIFF)).then_inc(PTm_copied, 1)
                    if u < N_DIFF:
                        unit_max(u + 1)
                    if u == N_DIFF:
                        dve.wait_ge(pv_done, 12 * t + N_DIFF)
                        nc.vector.tensor_copy(ya, OV[:, :]).then_inc(od_copied, 1)
                after(nc.vector.reciprocal(rsum[:, 8:16], psum_p[:, 8:16]))
                dve.wait_ge(pv_done, 12 * (t + 1))
                nc.vector.tensor_tensor(yb.rearrange("p (h d) -> p h d", h=8),
                                        OV[:, :].rearrange("p (h d) -> p h d", h=8),
                                        rsum[:, 8:16].unsqueeze(2).to_broadcast([P, 8, DH]),
                                        ALU.mult).then_inc(yb_ready, 1)
                dve.wait_ge(sq_ready, NKT + 2 * NKT + 4 * t + 3)
                after(nc.vector.tensor_reduce(ss[:, 0:4], ysq.rearrange("p (h d) -> p h d", h=4), AX.X, ALU.add))
                inverse_root(P, 4, DV)
                y3 = ya.rearrange("p (h d) -> p h d", h=4)
                nc.vector.tensor_tensor(y3, y3, rstd[:, 0:4].unsqueeze(2).to_broadcast([P, 4, DV]),
                                        ALU.mult).then_inc(ya_ready, 1)
                for b in range(2):
                    dve.wait_ge(yT_psum, 2 * t + b + 1)
                    dst = yT[:, b, :, :].rearrange("p k q -> p (k q)")
                    if b == 0:
                        nc.vector.tensor_scalar(dst, TR[:, :], small[:, K_SUB:K_SUB + 1], 1.0 - LAMBDA_INIT,
                                                ALU.mult, ALU.mult).then_inc(yT_ready, 1)
                    else:
                        nc.vector.tensor_copy(dst, TR[:, :]).then_inc(yT_ready, 1)
                for n in range(2):
                    dve.wait_ge(chunk_done, group_done(t, CH_B, 2 + n, 4))
                    nc.vector.scalar_tensor_tensor(out=tg[:, n, :], in0=tg[:, n, :], scalar=1.0, in1=bank(n),
                                                   op0=ALU.add, op1=ALU.mult)
                    after(nc.vector.scalar_tensor_tensor(out=tg[:, 2 + n, :], in0=tg[:, 2 + n, :], scalar=1.0,
                                                         in1=bank(2 + n), op0=ALU.add, op1=ALU.mult))
                    nc.vector.tensor_tensor(merged[:, n * W:(n + 1) * W], tg[:, n, :], tg[:, 2 + n, :],
                                            ALU.add).then_inc(merged_ready, 1)
                hb = hs[:, hsb(t), :]
                for n in range(2):
                    dve.wait_ge(chunk_done, group_done(t, CH_O, n))
                    if n == 0:
                        dve.wait_ge(x_in[hsb(t)], x_count(t))
                    nc.vector.scalar_tensor_tensor(out=hb[:, n * W:(n + 1) * W], in0=bank(2 + n), scalar=0.5,
                                                   in1=hb[:, n * W:(n + 1) * W], op0=ALU.mult,
                                                   op1=ALU.add).then_inc(hs_ready, 1)
                dve.wait_ge(sq_ready, NKT + 2 * NKT + 4 * t + 4)
                inverse_root(P, 1, D)
                nc.vector.scalar_tensor_tensor(out=h2[:, hsb(t), :], in0=hb, scalar=rstd[:, 0:1], in1=ffng[:, :],
                                               op0=ALU.mult, op1=ALU.mult).then_inc(h2_ready, 1)

                def top16(vals, inds, src, n, signal=None):
                    after(nc.vector.max(vals[:, 0:8], src))
                    nc.vector.max_index(inds[:, 0:8], vals[:, 0:8], src)
                    ins = nc.vector.match_replace(scrap[:, 0:n], vals[:, 0:8], src, LOWEST)
                    if signal is not None:
                        ins.then_inc(signal, 1)
                        dve.wait_ge(signal, 4 * t + nq + 1)
                    else:
                        after(ins)
                    after(nc.vector.max(vals[:, 8:16], scrap[:, 0:n]))
                    after(nc.vector.max_index(inds[:, 8:16], vals[:, 8:16], scrap[:, 0:n]))

                for nq in range(4):
                    dve.wait_ge(key_scores, 4 * t + nq + 1)
                    for j in range(4):
                        top16(top[:, 4 * nq + j, :], topi[:, 4 * nq + j, :], OV[:, j * P:(j + 1) * P], NKEYS,
                              keys_taken if j == 3 else None)
                    for h in (2 * nq, 2 * nq + 1):
                        after(nc.vector.tensor_tensor(cand.rearrange("p (a b) -> p a b", a=TOPK),
                                                      top[:, 2 * h, :].unsqueeze(2).to_broadcast([P, TOPK, TOPK]),
                                                      top[:, 2 * h + 1, :].unsqueeze(1).to_broadcast([P, TOPK, TOPK]),
                                                      ALU.add))
                        top16(best[:, h, :], posn[:, h, :], cand, TOPK * TOPK)
                g3 = gate[:, t % 2, :].rearrange("p (h k) -> p h k", h=PH)
                nc.vector.tensor_tensor(g3, best[:, :, :], best[:, :, 0:1].to_broadcast([P, PH, TOPK]),
                                        ALU.subtract).then_inc(gate_shift, 1)
                nc.vector.tensor_copy(topf[:, :, :], topi[:, :, :])
                nc.vector.tensor_scalar(posa[:, 0, :, :], posn[:, :, :], 4, None, ALU.logical_shift_right)
                after(nc.vector.tensor_scalar(posa[:, 1, :, :], posn[:, :, :], TOPK - 1, None, ALU.bitwise_and))
                after(nc.vector.tensor_copy(work[:, 256:512], work[:, 0:256].bitcast(U32)))
                if t == 0:
                    dve.wait_ge(iota_ready, 1)
                for c in range(2):
                    for h in range(PH):
                        ins = nc.vector.tensor_tensor(hot[:, h, :, :],
                                                posf[:, c, h, :].unsqueeze(2).to_broadcast([P, TOPK, TOPK]),
                                                iota16[:, :].unsqueeze(1).to_broadcast([P, TOPK, TOPK]), ALU.is_equal)
                    after(ins)
                    for h in range(PH):
                        ins = nc.vector.tensor_tensor(hot[:, h, :, :], hot[:, h, :, :],
                                                topf[:, 2 * h + c, :].unsqueeze(1).to_broadcast([P, TOPK, TOPK]),
                                                ALU.mult)
                    after(ins)
                    after(nc.vector.tensor_reduce(sel[:, c, :, :].rearrange("p h k -> p (h k)"),
                                                  hot.rearrange("p h k a -> p (h k) a"), AX.X, ALU.add))
                dve.wait_ge(gate_exp, t + 1)
                after(nc.vector.tensor_reduce(gsum[:, 0, :], g3, AX.X, ALU.add))
                after(nc.vector.reciprocal(gsum[:, 1, :], gsum[:, 0, :]))
                nc.vector.tensor_tensor(g3, g3, gsum[:, 1, :].unsqueeze(2).to_broadcast([P, PH, TOPK]), ALU.mult)
                nc.vector.scalar_tensor_tensor(out=idx[:, t % 2, :], in0=sel[:, 0, :, :].rearrange("p h k -> p (h k)"),
                                               scalar=float(NKEYS), in1=sel[:, 1, :, :].rearrange("p h k -> p (h k)"),
                                               op0=ALU.mult, op1=ALU.add).then_inc(route_ready, 1)
                dve.wait_ge(route_ready, t + 1)
                def weigh(e):
                    n = NE * t + e
                    dve.wait_ge(act_ready, n // 2 + 1)
                    w = e % (2 * RING)
                    nc.vector.tensor_tensor(wexp[:, w:w + 2], acts[:, w:w + 2], gate[:, t % 2, e:e + 2],
                                            ALU.mult).then_inc(wexp_ready, 1)

                for e in range(NE):
                    n = NE * t + e
                    dve.wait_ge(row_landed[e % RING], 16 * (n // RING + 1))
                    u_row = ring[:, e % RING, 0:D]
                    nc.vector.tensor_tensor_reduce(out=u_row, in0=u_row, in1=h2[:, hsb(t), :], scale=1.0, scalar=0.0,
                                                   op0=ALU.mult, op1=ALU.add,
                                                   accum_out=dots[:, e % (2 * RING):e % (2 * RING) + 1]).then_inc(dot_ready, 1)
                    if e % 2 == 0 and e >= 2:
                        weigh(e - 2)
                weigh(NE - 2)
                dve.wait_ge(rochunk_done, NE * (t + 1))
                nc.vector.tensor_tensor(hb, hb, Y[:, :], ALU.add).then_inc(out_ready, 1)

        @block.gpsimd
        def _(pool):
            nc.gpsimd.iota(iota16[:, :], pattern=[[1, TOPK]], base=0, channel_multiplier=0,
                           allow_small_or_imprecise_dtypes=True).then_inc(iota_ready, 1)
            for t in range(NT):
                pool.wait_ge(route_ready, t + 1)
                for e in range(NE):
                    n = NE * t + e
                    if n >= RING:
                        pool.wait_ge(rochunk_done, n - RING + 1)
                    pool.indirect_dma_start(ring[:, e % RING, :], None, experts[:, :],
                                            bass.IndirectOffsetOnAxis(ap=idx[:, t % 2, e:e + 1], axis=0)
                                            ).then_inc(row_landed[e % RING], 16)


def kernel(**inputs):
    import numpy as np
    import concourse.bacc as bacc
    from concourse.bass_utils import run_bass_kernel_spmd

    nc = bacc.Bacc("TRN2", target_bir_lowering=False, num_devices=1)

    def flat(name):
        return np.ascontiguousarray(np.asarray(inputs[name])[0])

    tri = (np.arange(P)[:, None] <= np.arange(P)[None, :]).astype(np.float32)
    col = np.arange(MASK_W)[None, :] - (SEQ - P)
    row = np.arange(P)[:, None]
    mask_f = np.where(col <= row, 0.0, MASKED)
    mask_d = np.where(col // CHUNK <= row // CHUNK, 0.0, MASKED)
    table = np.concatenate([np.eye(P), tri, mask_d, mask_f], axis=1).astype(np.float32)
    pos = np.concatenate([np.arange(SEQ) + N_META, np.arange(N_META), np.zeros(P - N_META)]).astype(np.float32)
    inv = np.float32(ROPE_THETA) ** (-np.arange(0, DH, 2, dtype=np.float32) / np.float32(DH))
    ang = pos[:, None] * inv[None, :].astype(np.float32)
    cos, sin = np.cos(ang), np.sin(ang)
    rope = np.concatenate([cos, cos, -sin, sin], axis=1).astype(np.float32)
    rope = np.ascontiguousarray(rope.reshape(NT + 1, P, 2 * DH).transpose(1, 0, 2))
    r = np.arange(P)
    lower = ((r >= 8) & (r < 16)).astype(np.float32)
    head = np.arange(N_FOX)[None, :]
    lsel = (r[:, None] == head).astype(np.float32)
    lneg = -(r[:, None] - 8 == head).astype(np.float32)

    two = lambda a: np.concatenate([a, a])[:, None]
    cols = np.concatenate([flat("norm_mix_g").reshape(KD, P).T, two(flat("fox_qnorm_g")), two(flat("fox_knorm_g")),
                           flat("diff_subln_g")[:, None], lower[:, None], 1.0 - lower[:, None], lsel, lneg],
                          axis=1).astype(np.float32)
    rows = np.concatenate([flat("norm_ffn_g"), flat("diff_qnorm_g"), flat("diff_knorm_g"),
                           flat("diff_lambda").reshape(-1)])
    arrays = {
        "x": np.ascontiguousarray(np.asarray(inputs["x"])[0]),
        "meta": np.ascontiguousarray(inputs["meta_tokens"]),
        "w_in": flat("w_in"), "b_gate": np.ascontiguousarray(inputs["b_gate"]),
        "b_forget": np.ascontiguousarray(inputs["b_forget"]),
        "w_bd": flat("w_branch_diff"), "w_bf": flat("w_branch_fox"), "w_out": flat("w_out"),
        "w_pq": flat("peer_w_q"),
        "subkeys_t": np.ascontiguousarray(flat("peer_subkeys").transpose(3, 0, 1, 2).reshape(P, 2 * PH, NKEYS)),
        "experts": np.concatenate([flat("peer_u"), flat("peer_v")], axis=1),
        "table": table, "cols": cols, "rows": np.tile(rows[None, :], (P, 1)), "rope": rope,
    }
    aps = {n: nc.dram_tensor(n, a.shape, mybir.dt.from_np(a.dtype), kind="ExternalInput").ap()
           for n, a in arrays.items()}
    out = nc.dram_tensor("out", (SEQ, D), F32, kind="ExternalOutput").ap()
    build(nc, **aps, out=out)
    res = run_bass_kernel_spmd(nc, [arrays], core_ids=[0])
    return res.results[0]["out"].reshape(1, SEQ, D)
```

```python
from contextlib import ExitStack

import concourse.bass as bass
from concourse import mybir

ALU = mybir.AluOpType
ACT = mybir.ActivationFunctionType
AX = mybir.AxisListType
F32 = mybir.dt.float32
BF16 = mybir.dt.bfloat16
U32 = mybir.dt.uint32

P = 128
D = 1024
KD = D // P
SEQ = 512
N_META = 16
NT = SEQ // P
KEYS = SEQ + N_META
CHUNK = 64
EPS = 1e-6
LAMBDA_INIT = 0.2
ROPE_THETA = 10000.0

DH, DV, DPAIRS = 64, 128, 4
N_DIFF, N_FOX = 4, 8
W = 512
DQ, DK, DVO, FQ, FK, FV = (i * W for i in range(6))
FF = 6 * W
GATES = FF + N_FOX

PH, NKEYS, TOPK = 8, 128, 16
NE = PH * TOPK
RING = 8
WSLOTS = 4
WK = 2
NDIAG = 4
V_ON_DVE = (1, 2, 3)
N_PE = NE * (4 - len(V_ON_DVE)) // 4
N_DVE = NE - N_PE
LOWEST = -3.0e38
MASKED = -1.0e30

C_ID, C_TRI, C_MASKD, C_MASKF, C_W = 0, P, 2 * P, 3 * P, 4 * P
K_MIXG, K_FQG, K_FKG, K_SUB, K_ROW0, K_ROW1, K_LSEL, K_LNEG = 0, 8, 9, 10, 11, 12, 13, 21
K_W = 29
R_FFNG, R_QG, R_KG, R_LAM, R_W = 0, D, D + 64, D + 128, D + 128 + 256


def build(nc, x, meta, w_in, b_gate, b_forget, w_bd, w_bf, w_out, w_pq, subkeys_t, experts,
          table, cols, rows, rope, out):
    with ExitStack() as ctx:
        def sb(name, shape, dt=F32):
            return ctx.enter_context(nc.sbuf_tensor(name, shape, dt))

        def sem(name):
            return ctx.enter_context(nc.semaphore(name))

        ring = sb("ring", [P, RING, 2 * D])
        hT = sb("hT", [P, KD, KEYS])
        kT = sb("kT", [P, 2, DPAIRS, KEYS])
        V = sb("V", [P, 2, NT + 1, W])
        wring = sb("wring", [P, WSLOTS, WK, W])
        hs = sb("hs", [P, 2, D])
        h2 = sb("h2", [P, 2, D])
        work = sb("work", [P, 6144])
        subk = sb("subk", [P, 2 * PH, NKEYS])
        ffng = sb("ffng", [P, D])
        ropeC = sb("ropeC", [P, 2, NT + 1, DH])
        ropeS = sb("ropeS", [P, 2, NT + 1, DH])
        ident = sb("ident", [P, 2 * P])
        ident_bf = sb("ident_bf", [P, P], BF16)
        mask_bf = sb("mask_bf", [P, 2, P], BF16)
        small = sb("small", [P, K_W])
        ones = sb("ones", [P, P])
        bgate = sb("bgate", [P, W])
        wf = sb("wf", [P, KD, N_FOX])
        bf = sb("bf", [1, N_FOX])
        logf = sb("logf", [P, NT + 1, N_FOX])
        cum2 = sb("cum2", [P, NT + 1, 2 * N_FOX])
        decR = sb("decR", [16, KEYS])
        cumT = sb("cumT", [16, SEQ])
        lamt = sb("lamt", [P, 8])
        ss = sb("ss", [P, 8])
        std = sb("std", [P, 8])
        rstd = sb("rstd", [P, 8])
        nmax = sb("nmax", [P, 16])
        psum_p = sb("psum_p", [P, 16])
        rsum = sb("rsum", [P, 16])
        iota16 = sb("iota16", [P, TOPK])
        gsum = sb("gsum", [P, 2, PH])
        idx = sb("idx", [P, 2, NE], U32)
        gate = sb("gate", [P, 2, NE])
        dots = sb("dots", [P, 2 * RING])
        acts = sb("acts", [P, 2 * RING])
        wexp = sb("wexp", [P, 2 * RING])
        diag = sb("diag", [P, NDIAG, P])

        xn = [work[:, 0:D], work[:, D:2 * D]]
        heads = [work[:, 0:W], work[:, 5120:5120 + W]]
        qT = [work[:, 512:1024].rearrange("p (j q) -> p j q", j=DPAIRS),
              work[:, 1024:1536].rearrange("p (j q) -> p j q", j=DPAIRS)]
        qraw = work[:, 1536:2048]
        qA = work[:, 2048:2560]
        probs = [work[:, 1536 + i * KEYS:1536 + (i + 1) * KEYS] for i in range(4)]
        PT = [work[:, 3648 + i * 640:3648 + (i + 1) * 640] for i in range(2)]
        ya, yb = work[:, 5120:5632], work[:, 5632:6144]
        ysq = work[:, 0:W]
        tg = work[:, 0:2048].rearrange("p (n w) -> p n w", n=4)
        merged = work[:, 2048:3072]
        mT = work[:, 3072:4096].rearrange("p (k q) -> p k q", k=KD)
        yT = work[:, 4096:5120].rearrange("p (b k q) -> p b k q", b=2, k=4)
        hsq = work[:, 5120:6144]
        h2T = work[:, 0:1024].rearrange("p (k q) -> p k q", k=KD)
        pq = work[:, 1024:2048].rearrange("p (b w) -> p b w", b=2)
        pqT = work[:, 2048:2560].rearrange("p (j q) -> p j q", j=4)
        scrap = work[:, 2560:2816]
        cand = work[:, 2816:3072]
        hot = work[:, 3072:3584].rearrange("p (h k a) -> p h k a", h=2, k=TOPK)

        decL = [work[0:16, 0:W].rearrange("p (h q) -> p h q", h=4),
                work[0:16, 5632:5632 + W].rearrange("p (h q) -> p h q", h=4)]

        def routing(at, dt, *dims):
            n = 1
            for d in dims:
                n *= d
            v = work[:, at:at + n] if dt is F32 else work[:, at:at + n].bitcast(dt)
            names = "abc"[:len(dims)]
            return v.rearrange(f"p ({' '.join(names)}) -> p {' '.join(names)}", **dict(zip(names, dims)))

        top = routing(5120, F32, 2 * PH, TOPK)
        topi = routing(5376, U32, 2 * PH, TOPK)
        topf = routing(5632, F32, 2 * PH, TOPK)
        best = routing(5888, F32, PH, TOPK)
        posn = routing(6016, U32, PH, TOPK)
        posa = routing(3584, U32, 2, 2, TOPK)
        posf = routing(3648, F32, 2, 2, TOPK)
        sel = routing(3712, F32, 2, 2, TOPK)

        SC = ctx.enter_context(nc.psum_tensor("SC", [P, 4 * W], F32))
        TR = ctx.enter_context(nc.psum_tensor("TR", [P, W], F32))
        OV = ctx.enter_context(nc.psum_tensor("OV", [P, W], F32))
        Y = ctx.enter_context(nc.psum_tensor("Y", [P, D], F32))

        def bank(i):
            return SC[:, i * W:(i + 1) * W]

        def meta_T(c):
            b = (c % 2) * 2 * W
            return SC[0:N_META, b + 640:b + 640 + P]

        consts_in = sem("consts_in")
        x_in = [sem("x_in0"), sem("x_in1")]
        w_in_sem = [sem(f"w_landed{i}") for i in range(WSLOTS)]
        chunk_done = sem("chunk_done")
        dve_step = sem("dve_step")
        act_step = sem("act_step")
        setup = sem("setup")
        iota_ready = sem("iota_ready")
        sq_ready = sem("sq_ready")
        var_ready = sem("var_ready")
        std_ready = sem("std_ready")
        xn_ready = sem("xn_ready")
        xT_ready = sem("xT_ready")
        hT_ready = sem("hT_ready")
        kv_ready = sem("kv_ready")
        heads_ready = sem("heads_ready")
        headsT_ready = sem("headsT_ready")
        qk_ready = sem("qk_ready")
        v_copied = sem("v_copied")
        f_ready = sem("f_ready")
        f_neg = sem("f_neg")
        f_soft = sem("f_soft")
        logf_ready = sem("logf_ready")
        cum_ready = sem("cum_ready")
        cum_copied = sem("cum_copied")
        cumT_ready = sem("cumT_ready")
        dec_ready = sem("dec_ready")
        lam_dots = sem("lam_dots")
        lam_exp = sem("lam_exp")
        scores_ready = sem("scores_ready")
        max_ready = sem("max_ready")
        exp_ready = sem("exp_ready")
        mix_ready = sem("mix_ready")
        PT_ready = sem("PT_ready")
        PT_copied = sem("PT_copied")
        PTm_copied = sem("PTm_copied")
        pv_done = sem("pv_done")
        od_copied = sem("od_copied")
        yb_ready = sem("yb_ready")
        ya_ready = sem("ya_ready")
        yT_psum = sem("yT_psum")
        yT_ready = sem("yT_ready")
        tanh_ready = sem("tanh_ready")
        merged_ready = sem("merged_ready")
        mT_psum = sem("mT_psum")
        mT_ready = sem("mT_ready")
        hs_ready = sem("hs_ready")
        h2_ready = sem("h2_ready")
        h2T_psum = sem("h2T_psum")
        h2T_ready = sem("h2T_ready")
        pq_copied = sem("pq_copied")
        pqT_psum = sem("pqT_psum")
        pqT_copied = sem("pqT_copied")
        key_scores = sem("key_scores")
        keys_taken = sem("keys_taken")
        gate_shift = sem("gate_shift")
        gate_exp = sem("gate_exp")
        route_ready = sem("route_ready")
        row_landed = [sem(f"row_landed{i}") for i in range(RING)]
        dot_ready = sem("dot_ready")
        act_ready = sem("act_ready")
        wexp_ready = sem("wexp_ready")
        diag_ready = sem("diag_ready")
        row_used = sem("row_used")
        row_used_dve = sem("row_used_dve")
        out_ready = sem("out_ready")
        out_stored = sem("out_stored")

        N_CONST = 10
        KV = [DK, FK, DVO, FV]
        tiles = [(s * P, P) for s in range(NT)] + [(SEQ, N_META)]
        NKT = len(tiles)

        PASSES = [(NT, 0), (1, 2, 3)]
        KV = [DK, FK, DVO, FV]
        front = ([("q", 0), ("q", 1), ("qT", 0), ("qT", 1)] + [("unit", u) for u in range(12)] + [("heads_out", 0)]
                 + [("gate", n) for n in range(4)] + [("yT", 0), ("yT", 1)]
                 + [("branch", n) for n in range(4)] + [("merge", 0), ("out", 0), ("out", 1), ("h2", 0), ("h2T", 0)]
                 + [p for n in range(4) for p in (("pq", n), ("keys", n), ("route", n))])
        cost = {"kv": 20, "kT": 4, "forget": 8, "q": 8, "qT": 3, "unit": 5, "heads_out": 5, "gate": 7, "yT": 2,
                "branch": 4, "merge": 5, "out": 7, "h2": 4, "h2T": 3, "pq": 7, "keys": 9, "route": 8}

        def kv_pieces(p):
            return [("kv", (p, 0)), ("kT", (p, 0)), ("kv", (p, 1)), ("kT", (p, 1)), ("kv", (p, 2)), ("kv", (p, 3)),
                    ("forget", p)]

        def experts_and_front(t):
            pieces = []
            if t + 1 < NT:
                pieces = (kv_pieces(1) if t == 0 else []) + front
            total, done, e, order = sum(cost[k] for k, _ in pieces), 0, 0, []
            for k, a in pieces:
                done += cost[k]
                order.append((k, t + 1, a))
                e1 = min(NE, 2 * (NE * done // total // 2))
                if e1 > e:
                    order.append(("experts", t, (e, e1)))
                    e = e1
            if e < NE:
                order.append(("experts", t, (e, NE)))
            return order + [("finish", t, 0)]

        order = [(k, 0, a) for k, a in kv_pieces(0) + front]
        for t in range(NT):
            order += experts_and_front(t)

        all_chunks, first_chunk = [], {}

        def add_group(key, w, c0, k_tiles):
            v = w.rearrange("(k p) n -> p k n", p=P)
            first_chunk[key] = len(all_chunks)
            all_chunks.extend(v[:, k:k + WK, c0:c0 + W] for k in range(0, k_tiles, WK))

        for k, t, a in order:
            if k == "kv":
                add_group((k, a), w_in, KV[a[1]], KD)
            elif k == "q":
                add_group((k, t, a), w_in, (DQ, FQ)[a], KD)
            elif k == "gate":
                add_group((k, t, a), w_in, GATES + a * W, KD)
            elif k == "branch":
                add_group((k, t, a), (w_bd, w_bf)[a // 2], (a % 2) * W, 4)
            elif k == "out":
                add_group((k, t, a), w_out, a * W, KD)
            elif k == "pq":
                add_group((k, t, a), w_pq, a * W, KD)

        def group_done(k_tiles, *key):
            return first_chunk[key] + k_tiles // WK

        def kv_item(p, g, i):
            return (0 if p == 0 else 4 * len(PASSES[0])) + g * len(PASSES[p]) + i

        def kv_bank(p, g, i):
            return kv_item(p, g, i) % 4

        head_items = []
        for k, t, a in order:
            if k == "kv" and a[1] < 2:
                head_items += [("k", a[0], a[1], i) for i in range(len(PASSES[a[0]]))]
            elif k == "q":
                head_items.append(("q", t, a))
        head_no = {key: n for n, key in enumerate(head_items)}
        V_ITEMS = [0, 2 * len(PASSES[0])]

        def wait_kv(eng, p, g, i):
            if i < len(PASSES[p]) - 1:
                before = 0 if p == 0 else 4 * (len(PASSES[0]) - 1)
                eng.wait_ge(kv_ready, before + g * (len(PASSES[p]) - 1) + i + 1)
            else:
                eng.wait_ge(chunk_done, group_done(KD, "kv", (p, g)))

        def pe_count(n):
            return n // 4 * (4 - len(V_ON_DVE)) + len([j for j in range(n % 4) if j not in V_ON_DVE])

        def dve_count(n):
            return n - pe_count(n)

        N_LOADS = 14
        CONSTS = 16 * N_LOADS

        def hsb(t):
            return (NKT + 1 + t) % 2

        def x_count(t):
            i = NKT + 1 + t
            return 16 * len([j for j in [*range(NKT), *range(NKT + 1, i + 1)] if j % 2 == i % 2])

        token_order = [NT, 0, 1, 2, 3]
        block = ctx.enter_context(nc.Block())

        @block.sync
        def _(sp):
            def load_x(i, t):
                c0, r = tiles[t]
                src = x[c0:c0 + r, :] if t < NT else meta
                sp.dma_start(hs[0:r, i % 2, :], src).then_inc(x_in[i % 2], 16)

            def load_chunk(n):
                if n >= WSLOTS:
                    sp.wait_ge(chunk_done, n - WSLOTS + 1)
                sp.dma_start(wring[:, n % WSLOTS, :, :], all_chunks[n]).then_inc(w_in_sem[n % WSLOTS], 16)

            load_x(0, token_order[0])
            load_x(1, token_order[1])
            consts = [(small[:, :], cols), (ident[:, :], table[:, 0:2 * P]),
                      (work[:, 2048:2048 + 2 * P], table[:, 2 * P:C_W]),
                      (ropeC[:, 0, :, :], rope[:, :, 0:DH]), (ropeS[:, 0, :, :], rope[:, :, DH:2 * DH]),
                      (work[:, 4096:4096 + R_W - D], rows[:, D:R_W]), (ffng[:, :], rows[:, 0:D]),
                      (subk[:, :, :], subkeys_t),
                      (wf[:, :, :], w_in[:, FF:FF + N_FOX].rearrange("(k p) n -> p k n", p=P)),
                      (bf[:, :], b_forget)]
            consts += [(bgate[32 * n:32 * n + 1, :], b_gate[:, n * W:(n + 1) * W]) for n in range(4)]
            assert len(consts) == N_LOADS
            for dst, src in consts:
                sp.dma_start(dst, src).then_inc(consts_in, 16)
            for n in range(WSLOTS):
                load_chunk(n)
            for i in range(2, NKT):
                sp.wait_ge(xn_ready, i - 1)
                load_x(i, token_order[i])
            sp.wait_ge(xn_ready, NKT)
            load_x(NKT + 1, 0)
            n = WSLOTS
            for t in range(NT):
                while n < group_done(KD, "pq", t, 3):
                    load_chunk(n)
                    n += 1
                if t >= 1:
                    sp.wait_ge(out_ready, t)
                    sp.dma_start(out[(t - 1) * P:t * P, :], hs[:, hsb(t - 1), :]).then_inc(out_stored, 16)
                    sp.wait_ge(out_stored, 16 * t)
                if t + 1 < NT:
                    load_x(NKT + 2 + t, t + 1)
            sp.wait_ge(out_ready, NT)
            sp.dma_start(out[(NT - 1) * P:NT * P, :], hs[:, hsb(NT - 1), :]).then_inc(out_stored, 16)
            sp.wait_ge(out_stored, 16 * NT)

        @block.tensor
        def _(pe):
            idm = ident[:, 0:P]
            tri = ident[:, P:2 * P]

            def use_chunks(key, k_tiles, lhs, acc, bias=None):
                if bias is not None:
                    nc.tensor.matmul(acc, *bias, start=True, stop=False)
                for j in range(k_tiles // WK):
                    n = first_chunk[key] + j
                    pe.wait_ge(w_in_sem[n % WSLOTS], 16 * (n // WSLOTS + 1))
                    for i in range(WK):
                        k = j * WK + i
                        mm = nc.tensor.matmul(acc, lhs(k), wring[:, n % WSLOTS, i, :],
                                              start=(k == 0 and bias is None), stop=(k == k_tiles - 1))
                    mm.then_inc(chunk_done, 1)

            def turn(dst, src, r=P):
                for j in range(src.shape[-1] // P):
                    mm = nc.tensor.transpose(dst[:, j * P:j * P + r], src[0:r, j * P:(j + 1) * P], ident[0:r, 0:r])
                return mm

            def headsT(key, r):
                i = head_no[key]
                pe.wait_ge(heads_ready, i + 1)
                if i >= 1:
                    pe.wait_ge(qk_ready, i)
                turn(TR, heads[i % 2], r).then_inc(headsT_ready, 1)

            def kv(t, a):
                p, g = a
                key_tiles = PASSES[p]
                for j in range(KD // WK):
                    n = first_chunk[("kv", a)] + j
                    pe.wait_ge(w_in_sem[n % WSLOTS], 16 * (n // WSLOTS + 1))
                    for i, s in enumerate(key_tiles):
                        c0, r = tiles[s]
                        m = kv_item(p, g, i)
                        first = kv_item(p, 0, 0)
                        if j == 0 and m - 4 >= first:
                            g4, i4 = divmod(m - 4 - first, len(key_tiles))
                            if g4 < 2:
                                pe.wait_ge(heads_ready, head_no[("k", p, g4, i4)] + 1)
                            else:
                                pe.wait_ge(v_copied, V_ITEMS[p] + (g4 - 2) * len(key_tiles) + i4 + 1)
                        for b in range(WK):
                            k = j * WK + b
                            mm = nc.tensor.matmul(bank(m % 4)[0:r, :], hT[:, k, c0:c0 + r],
                                                  wring[:, n % WSLOTS, b, :], start=(k == 0), stop=(k == KD - 1))
                        if i == len(key_tiles) - 1:
                            mm.then_inc(chunk_done, 1)
                        elif j == KD // WK - 1:
                            mm.then_inc(kv_ready, 1)

            def kT_(t, a):
                p, g = a
                for i, s in enumerate(PASSES[p]):
                    headsT(("k", p, g, i), tiles[s][1])

            def forget(t, p):
                pe.wait_ge(qk_ready, head_no[("k", p, 1, len(PASSES[p]) - 1)] + 1)
                for s in PASSES[p]:
                    c0, r = tiles[s]
                    o = TR[0:r, s * N_FOX:(s + 1) * N_FOX]
                    nc.tensor.matmul(o, ones[0:1, 0:r], bf[:, :], start=True, stop=False)
                    for k in range(KD):
                        mm = nc.tensor.matmul(o, hT[:, k, c0:c0 + r], wf[:, k, :], start=False, stop=(k == KD - 1))
                mm.then_inc(f_ready, 1)
                pe.wait_ge(logf_ready, p + 1)
                for s in PASSES[p]:
                    r = tiles[s][1]
                    o = TR[0:r, s * N_FOX:(s + 1) * N_FOX]
                    if s == NT:
                        mm = nc.tensor.matmul(o, tri[0:N_META, 0:N_META], logf[0:N_META, NT, :], start=True, stop=True)
                        continue
                    nc.tensor.matmul(o, ones[0:N_META, :], logf[0:N_META, NT, :], start=True, stop=False)
                    for b in range(s):
                        nc.tensor.matmul(o, ones[:, :], logf[:, b, :], start=False, stop=False)
                    mm = nc.tensor.matmul(o, tri, logf[:, s, :], start=False, stop=True)
                mm.then_inc(cum_ready, 1)
                pe.wait_ge(cum_copied, p + 1)
                for i, s in enumerate(PASSES[p]):
                    r = tiles[s][1]
                    mm = nc.tensor.transpose(TR[0:16, i * P:i * P + r], cum2[0:r, s, :], ident[0:r, 0:r])
                mm.then_inc(cumT_ready, 1)

            def q(t, g):
                if g == 0 and t < 2:
                    pe.wait_ge(v_copied, 2 * sum(len(x_) for x_ in PASSES[0:t + 1]))
                use_chunks(("q", t, g), KD, lambda k: hT[:, k, t * P:(t + 1) * P], bank(g))

            def qT_(t, g):
                headsT(("q", t, g), P)

            def scores(t, c):
                n, nk = 16 * t + c, (t + 1) * P
                if c >= 2:
                    pe.wait_ge(exp_ready, n - 1)
                if c >= 9 or (c % 2 == 1 and c >= 3):
                    pe.wait_ge(PTm_copied, 12 * t + (c - 5 if c >= 9 else (c - 1) // 2))
                fox = c >= 2 * N_DIFF
                g = c - 8 if fox else (c % 2) * N_DIFF + c // 2
                lo = DH * (g % 2)
                query = qT[fox][lo:lo + DH, g // 2, :]
                b = (c % 2) * 2 * W
                acc, accm = SC[:, b:b + nk], SC[:, b + nk:b + nk + N_META]
                nc.tensor.matmul(acc, query, kT[lo:lo + DH, int(fox), g // 2, 0:nk], start=True, stop=False)
                if fox:
                    nc.tensor.matmul(acc, decL[g // 4][:, g % 4, :], decR[:, 0:nk], start=False, stop=False)
                nc.tensor.matmul(acc[:, nk - P:nk], ident_bf[:, :], mask_bf[:, int(fox), :], start=False, stop=True)
                mm = nc.tensor.matmul(accm, query, kT[lo:lo + DH, int(fox), g // 2, SEQ:KEYS], start=True,
                                      stop=not fox)
                if fox:
                    mm = nc.tensor.matmul(accm, decL[g // 4][:, g % 4, :], decR[:, SEQ:KEYS], start=False, stop=True)
                mm.then_inc(scores_ready, 1)

            def probsT(t, u):
                c = 2 * u + 1 if u < N_DIFF else u + N_DIFF
                if u < N_DIFF:
                    pe.wait_ge(mix_ready, N_DIFF * t + u + 1)
                else:
                    pe.wait_ge(exp_ready, 16 * t + c + 1)
                if u >= 1:
                    pe.wait_ge(PT_copied, 12 * t + u)
                    pe.wait_ge(PTm_copied, 12 * t + u)
                pr, nk = probs[c % 4], (t + 1) * P
                turn(TR, pr[:, 0:nk])
                nc.tensor.transpose(meta_T(c), pr[:, nk:nk + N_META], idm).then_inc(PT_ready, 1)

            def pv(t, u):
                n = 12 * t + u
                pe.wait_ge(PT_copied, n + 1)
                pe.wait_ge(PTm_copied, n + 1)
                if u == N_DIFF:
                    pe.wait_ge(od_copied, t + 1)
                fox = u >= N_DIFF
                wv = DH if fox else DV
                h = u - N_DIFF if fox else u
                o = OV[:, h * wv:(h + 1) * wv]
                pt = PT[u % 2]
                for s in range(t + 1):
                    nc.tensor.matmul(o, pt[:, s * P:(s + 1) * P], V[:, int(fox), s, h * wv:(h + 1) * wv],
                                     start=(s == 0), stop=False)
                nc.tensor.matmul(o, pt[0:N_META, SEQ:SEQ + P], V[0:N_META, int(fox), NT, h * wv:(h + 1) * wv],
                                 start=False, stop=True).then_inc(pv_done, 1)

            def unit(t, u):
                if u == 0:
                    pe.wait_ge(qk_ready, head_no[("q", t, 1)] + 1)
                    pe.wait_ge(dec_ready, t + 1 + (2 if t else 1))
                    if t >= 1:
                        pe.wait_ge(keys_taken, 4 * t)
                if u < N_DIFF:
                    scores(t, 2 * u)
                    scores(t, 2 * u + 1)
                    if u >= 1:
                        pv(t, u - 1)
                    probsT(t, u)
                    return
                if u == N_DIFF:
                    scores(t, u + N_DIFF)
                    pv(t, u - 1)
                if u + 1 < 12:
                    scores(t, u + 1 + N_DIFF)
                probsT(t, u)
                if u > N_DIFF:
                    pv(t, u - 1)

            def heads_out(t, _):
                pv(t, 11)

            def gate_(t, n):
                use_chunks(("gate", t, n), KD, lambda k: hT[:, k, t * P:(t + 1) * P], bank(n),
                           (ones[32 * n:32 * n + 1, :], bgate[32 * n:32 * n + 1, :]))

            def yT_(t, b):
                if b == 0:
                    pe.wait_ge(ya_ready, t + 1)
                else:
                    pe.wait_ge(yb_ready, t + 1)
                    pe.wait_ge(yT_ready, 2 * t + 1)
                turn(TR, (ya, yb)[b]).then_inc(yT_psum, 1)

            def branch(t, n):
                b = n // 2
                pe.wait_ge(yT_ready, 2 * t + b + 1)
                pe.wait_ge(tanh_ready, 4 * t + n + 1)
                use_chunks(("branch", t, n), 4, lambda k: yT[:, b, k, :], bank(n))

            def merge(t, _):
                pe.wait_ge(merged_ready, 2 * t + 2)
                turn(SC, merged).then_inc(mT_psum, 1)

            def out_(t, n):
                pe.wait_ge(mT_ready, t + 1)
                use_chunks(("out", t, n), KD, lambda k: mT[:, k, :], bank(2 + n))

            def h2T_(t, _):
                pe.wait_ge(h2_ready, t + 1)
                turn(SC, h2[:, hsb(t), :]).then_inc(h2T_psum, 1)

            def pq_(t, n):
                pe.wait_ge(h2T_ready, t + 1)
                if n >= 2:
                    pe.wait_ge(pq_copied, 4 * t + n - 1)
                use_chunks(("pq", t, n), KD, lambda k: h2T[:, k, :], bank(2 + n % 2))

            def keys(t, n):
                m = 4 * t + n
                pe.wait_ge(pq_copied, m + 1)
                turn(TR, pq[:, n % 2, :]).then_inc(pqT_psum, 1)
                pe.wait_ge(pqT_copied, m + 1)
                if m >= 1:
                    pe.wait_ge(keys_taken, m)
                for j in range(4):
                    mm = nc.tensor.matmul(OV[:, j * P:(j + 1) * P], pqT[:, j, :], subk[:, 4 * n + j, :],
                                          start=True, stop=True)
                mm.then_inc(key_scores, 1)

            def experts_(t, span):
                for e in range(*span):
                    if e % 4 in V_ON_DVE:
                        continue
                    if e == 0 and t >= 1:
                        pe.wait_ge(out_ready, t)
                    n = N_PE * t + pe_count(e)
                    pe.wait_ge(diag_ready, n + 1)
                    for i in range(2):
                        mm = nc.tensor.matmul(Y[:, i * W:(i + 1) * W], diag[:, n % NDIAG, :],
                                              ring[:, e % RING, D + i * W:D + (i + 1) * W],
                                              start=(e == 0), stop=(pe_count(e) == N_PE - 1))
                    mm.then_inc(row_used, 1)

            pe.wait_ge(consts_in, CONSTS)
            for i, s in enumerate(token_order):
                r = tiles[s][1]
                pe.wait_ge(xn_ready, i + 1)
                if i >= 2:
                    pe.wait_ge(hT_ready, i - 1)
                turn(SC[:, (i % 2) * D:(i % 2 + 1) * D], xn[i % 2], r).then_inc(xT_ready, 1)
            pe.wait_ge(hT_ready, NKT)
            pe.wait_ge(setup, 1)
            work_of = {"kv": kv, "kT": kT_, "forget": forget, "q": q, "qT": qT_, "unit": unit, "heads_out": heads_out,
                       "gate": gate_, "yT": yT_, "branch": branch, "merge": merge, "out": out_, "h2T": h2T_,
                       "pq": pq_, "keys": keys, "experts": experts_}
            for k, t, a in order:
                if k in work_of:
                    work_of[k](t, a)

        @block.scalar
        def _(act):
            steps, roots = [0], [0]

            def after(ins):
                steps[0] += 1
                ins.then_inc(act_step, 1)
                act.wait_ge(act_step, steps[0])

            def squares(dst, src, acc=None):
                nc.scalar.activation(dst, src, ACT.Square, accum_out=acc).then_inc(sq_ready, 1)

            def root(r, n):
                roots[0] += 1
                act.wait_ge(var_ready, roots[0])
                nc.scalar.activation(std[0:r, 0:n], ss[0:r, 0:n], ACT.Sqrt).then_inc(std_ready, 1)

            def copy(dst, src, signal):
                nc.scalar.activation(dst, src, ACT.Copy).then_inc(signal, 1)

            def head_squares(key, src, r):
                if head_no[key] >= 1:
                    act.wait_ge(heads_ready, head_no[key])
                squares(qA[0:r, :], src[0:r, :])
                root(r, 8)

            def kv(t, a):
                p, g = a
                for i, s in enumerate(PASSES[p]):
                    r = tiles[s][1]
                    if g < 2 and i >= 2:
                        continue
                    wait_kv(act, p, g, i)
                    src = bank(kv_bank(p, g, i))
                    if g < 2:
                        head_squares(("k", p, g, i), src, r)
                    else:
                        copy(V[0:r, g - 2, s, :], src[0:r, :], v_copied)

            def kT_(t, a):
                p, g = a
                if len(PASSES[p]) > 2:
                    wait_kv(act, p, g, 2)
                    head_squares(("k", p, g, 2), bank(kv_bank(p, g, 2)), P)

            def forget(t, p):
                act.wait_ge(f_neg, p + 1)
                for s in PASSES[p]:
                    r = tiles[s][1]
                    ins = nc.scalar.activation(cum2[0:r, s, 0:8], cum2[0:r, s, 8:16], ACT.Exp)
                after(ins)
                for s in PASSES[p]:
                    r = tiles[s][1]
                    ins = nc.scalar.activation(cum2[0:r, s, 0:8], cum2[0:r, s, 0:8], ACT.Ln, bias=1.0)
                ins.then_inc(f_soft, 1)

            def q(t, g):
                act.wait_ge(chunk_done, group_done(KD, "q", t, g))
                head_squares(("q", t, g), bank(g), P)

            def exps(t, c):
                n = 16 * t + c
                act.wait_ge(max_ready, n + 1)
                if c >= 4:
                    v = c - 4
                    act.wait_ge(PT_ready, 12 * t + (v // 2 if v < 8 else v - 4) + 1)
                b, width = (c % 2) * 2 * W, (t + 1) * P + N_META
                nc.scalar.activation(probs[c % 4][:, 0:width], SC[:, b:b + width], ACT.Exp, bias=nmax[:, c:c + 1],
                                     accum_out=psum_p[:, c:c + 1]).then_inc(exp_ready, 1)

            def unit(t, u):
                if u < N_DIFF:
                    exps(t, 2 * u)
                    exps(t, 2 * u + 1)
                else:
                    if u == N_DIFF:
                        exps(t, u + N_DIFF)
                    if u + 1 < 12:
                        exps(t, u + 1 + N_DIFF)
                n = 12 * t + u
                act.wait_ge(PT_ready, n + 1)
                if n >= 2:
                    act.wait_ge(pv_done, n - 1)
                copy(PT[u % 2][:, 0:(t + 1) * P], TR[:, 0:(t + 1) * P], PT_copied)

            def heads_out(t, _):
                act.wait_ge(od_copied, t + 1)
                squares(ysq, ya)
                root(P, 4)

            def gate_(t, n):
                act.wait_ge(ya_ready, t + 1)
                act.wait_ge(chunk_done, group_done(KD, "gate", t, n))
                nc.scalar.activation(tg[:, n, :], bank(n), ACT.Tanh, scale=0.5).then_inc(tanh_ready, 1)

            def merge(t, _):
                act.wait_ge(mT_psum, t + 1)
                copy(mT.rearrange("p k q -> p (k q)"), SC[:, 0:D], mT_ready)

            def h2_(t, _):
                act.wait_ge(hs_ready, 2 * t + 2)
                squares(hsq, hs[:, hsb(t), :], ss[:, 0:1])
                root(P, 1)

            def h2T_(t, _):
                act.wait_ge(h2T_psum, t + 1)
                copy(h2T.rearrange("p k q -> p (k q)"), SC[:, 0:D], h2T_ready)

            def pq_(t, n):
                act.wait_ge(chunk_done, group_done(KD, "pq", t, n))
                copy(pq[:, n % 2, :], bank(2 + n % 2), pq_copied)

            def keys(t, n):
                m = 4 * t + n
                act.wait_ge(pqT_psum, m + 1)
                if m >= 1:
                    act.wait_ge(key_scores, m)
                copy(pqT.rearrange("p j q -> p (j q)"), TR[:, :], pqT_copied)

            def route(t, n):
                m = 4 * t + n
                act.wait_ge(gate_shift, m + 1)
                g_ = gate[:, t % 2, n * 2 * TOPK:(n + 1) * 2 * TOPK]
                nc.scalar.activation(g_, g_, ACT.Exp).then_inc(gate_exp, 1)

            def experts_(t, span):
                for e in range(*span, 2):
                    act.wait_ge(dot_ready, NE * t + e + 2)
                    w = e % (2 * RING)
                    nc.scalar.activation(acts[:, w:w + 2], dots[:, w:w + 2], ACT.Gelu).then_inc(act_ready, 1)
                    act.wait_ge(wexp_ready, (NE * t + e) // 2 + 1)
                    for j in (e, e + 1):
                        if j % 4 in V_ON_DVE:
                            continue
                        n = N_PE * t + pe_count(j)
                        if n >= NDIAG:
                            act.wait_ge(row_used, n - NDIAG + 1)
                        w = j % (2 * RING)
                        nc.scalar.activation(diag[:, n % NDIAG, :], ident[:, 0:P], ACT.Copy,
                                             scale=wexp[:, w:w + 1]).then_inc(diag_ready, 1)

            act.wait_ge(lam_dots, 2)
            nc.scalar.activation(lamt[:, 2:4], lamt[:, 0:2], ACT.Exp).then_inc(lam_exp, 1)
            for i, s in enumerate(token_order):
                r = tiles[s][1]
                act.wait_ge(x_in[i % 2], 16 * (i // 2 + 1))
                if i >= 1:
                    act.wait_ge(xn_ready, i)
                squares(ring[0:r, i, 0:D], hs[0:r, i % 2, :], ss[0:r, 0:1])
                root(r, 1)
            work_of = {"kv": kv, "kT": kT_, "forget": forget, "q": q, "unit": unit, "heads_out": heads_out, "gate": gate_,
                       "merge": merge, "h2": h2_, "h2T": h2T_, "pq": pq_, "keys": keys, "route": route,
                       "experts": experts_}
            for k, t, a in order:
                if k in work_of:
                    work_of[k](t, a)

        @block.vector
        def _(dve):
            steps, sums = [0], [0]

            def after(ins):
                steps[0] += 1
                ins.then_inc(dve_step, 1)
                dve.wait_ge(dve_step, steps[0])

            def wait_squares():
                sums[0] += 1
                dve.wait_ge(sq_ready, sums[0])

            def inverse_root(r, n, width, scale=None):
                nc.vector.tensor_scalar(ss[0:r, 0:n], ss[0:r, 0:n], 1.0 / width, EPS, ALU.mult,
                                        ALU.add).then_inc(var_ready, 1)
                dve.wait_ge(std_ready, sums[0])
                after(nc.vector.reciprocal(rstd[0:r, 0:n], std[0:r, 0:n]))
                if scale is not None:
                    after(nc.vector.tensor_scalar(rstd[0:r, 0:n], rstd[0:r, 0:n], scale, None, ALU.mult))

            v3 = lambda a: a.rearrange("p (g d) -> p g d", g=8)

            def norm_heads(key, r, psum, which, tile, scale):
                i = head_no[key]
                wait_squares()
                after(nc.vector.tensor_reduce(ss[0:r, 0:8], v3(qA[0:r, :]), AX.X, ALU.add))
                inverse_root(r, 8, DH, scale)
                rb = rstd[0:r, 0:8].unsqueeze(2).to_broadcast([r, 8, DH])
                hd = heads[i % 2]
                if i >= 2:
                    dve.wait_ge(headsT_ready, i - 1)
                if which is None:
                    nc.vector.tensor_tensor(v3(hd[0:r, :]), v3(psum[0:r, :]), rb, ALU.mult).then_inc(heads_ready, 1)
                    return
                after(nc.vector.tensor_tensor(v3(qraw[0:r, :]), v3(psum[0:r, :]), rb, ALU.mult))
                C = ropeC[0:r, which, tile, :].unsqueeze(1).to_broadcast([r, 8, DH])
                S = ropeS[0:r, which, tile, :]
                nc.vector.tensor_tensor(v3(hd[0:r, :]), v3(qraw[0:r, :]), C, ALU.mult)
                H = DH // 2
                for lo, src in ((0, H), (H, 0)):
                    ins = nc.vector.tensor_tensor(v3(qA[0:r, :])[:, :, lo:lo + H], v3(qraw[0:r, :])[:, :, src:src + H],
                                                  S[:, lo:lo + H].unsqueeze(1).to_broadcast([r, 8, H]), ALU.mult)
                after(ins)
                nc.vector.tensor_tensor(hd[0:r, :], hd[0:r, :], qA[0:r, :], ALU.add).then_inc(heads_ready, 1)

            def put_T(key, dst, r, gain):
                dve.wait_ge(headsT_ready, head_no[key] + 1)
                src = TR[:, :].rearrange("p (j q) -> p j q", j=DPAIRS)[:, :, 0:r]
                if gain is None:
                    nc.vector.tensor_copy(dst, src).then_inc(qk_ready, 1)
                else:
                    nc.vector.tensor_scalar(dst, src, gain, None, ALU.mult).then_inc(qk_ready, 1)

            def kv(t, a):
                p, g = a
                if g < 2:
                    for i, s in enumerate(PASSES[p]):
                        if i >= 2:
                            continue
                        norm_heads(("k", p, g, i), tiles[s][1], bank(kv_bank(p, g, i)), 1 if g == 0 else None, s, None)

            def kT_(t, a):
                p, g = a
                for i, s in enumerate(PASSES[p]):
                    c0, r = tiles[s]
                    put_T(("k", p, g, i), kT[:, g, :, c0:c0 + r], r, None if g == 0 else small[:, K_FKG:K_FKG + 1])
                    if i == 0 and len(PASSES[p]) > 2:
                        s2 = PASSES[p][2]
                        norm_heads(("k", p, g, 2), P, bank(kv_bank(p, g, 2)), 1 if g == 0 else None, s2, None)

            def forget(t, p):
                dve.wait_ge(f_ready, p + 1)
                for s in PASSES[p]:
                    r = tiles[s][1]
                    z = TR[0:r, s * N_FOX:(s + 1) * N_FOX]
                    nc.vector.tensor_scalar(logf[0:r, s, :], z, 0.0, None, ALU.min)
                    after(nc.vector.tensor_scalar(cum2[0:r, s, 8:16], z, 0.0, None, ALU.max))
                    ins = nc.vector.tensor_tensor(cum2[0:r, s, 8:16], logf[0:r, s, :], cum2[0:r, s, 8:16],
                                                  ALU.subtract)
                ins.then_inc(f_neg, 1)
                dve.wait_ge(f_soft, p + 1)
                for s in PASSES[p]:
                    r = tiles[s][1]
                    ins = nc.vector.tensor_tensor(logf[0:r, s, :], logf[0:r, s, :], cum2[0:r, s, 0:8], ALU.subtract)
                ins.then_inc(logf_ready, 1)
                dve.wait_ge(cum_ready, p + 1)
                for s in PASSES[p]:
                    r = tiles[s][1]
                    for j in range(2):
                        ins = nc.vector.tensor_copy(cum2[0:r, s, 8 * j:8 * j + 8], TR[0:r, s * N_FOX:(s + 1) * N_FOX])
                ins.then_inc(cum_copied, 1)
                dve.wait_ge(cumT_ready, p + 1)
                for i, s in enumerate(PASSES[p]):
                    c0, r = tiles[s]
                    src = TR[0:16, i * P:i * P + r]
                    ins = nc.vector.tensor_scalar(decR[:, c0:c0 + r], src, small[0:16, K_ROW0:K_ROW0 + 1],
                                                  small[0:16, K_ROW1:K_ROW1 + 1], ALU.mult, ALU.add)
                    if s < NT:
                        ins = nc.vector.tensor_copy(cumT[:, c0:c0 + r], src)
                ins.then_inc(dec_ready, 1)

            def q(t, g):
                norm_heads(("q", t, g), P, bank(g), 0 if g == 0 else None, t, DH ** -0.5)

            def qT_(t, g):
                put_T(("q", t, g), qT[g], P, None if g == 0 else small[:, K_FQG:K_FQG + 1])
                if g == 1:
                    dve.wait_ge(dec_ready, t + (2 if t else 1))
                    for h in range(N_FOX):
                        ins = nc.vector.tensor_scalar(decL[h // 4][:, h % 4, :], cumT[:, t * P:(t + 1) * P],
                                                      small[0:16, K_LSEL + h:K_LSEL + h + 1],
                                                      small[0:16, K_LNEG + h:K_LNEG + h + 1], ALU.mult, ALU.add)
                    ins.then_inc(dec_ready, 1)

            def row_max(t, c):
                dve.wait_ge(scores_ready, 16 * t + c + 1)
                b = (c % 2) * 2 * W
                nc.vector.tensor_reduce(nmax[:, c:c + 1], SC[:, b:b + (t + 1) * P + N_META], AX.X, ALU.max,
                                        negate=True).then_inc(max_ready, 1)

            def unit(t, u):
                width = (t + 1) * P + N_META
                if u < N_DIFF:
                    row_max(t, 2 * u)
                    row_max(t, 2 * u + 1)
                    c = 2 * u
                    p0, p1 = probs[c % 4][:, 0:width], probs[c % 4 + 1][:, 0:width]
                    dve.wait_ge(exp_ready, 16 * t + c + 2)
                    after(nc.vector.reciprocal(rsum[:, c:c + 2], psum_p[:, c:c + 2]))
                    nc.vector.tensor_scalar(p0, p0, rsum[:, c:c + 1], None, ALU.mult)
                    after(nc.vector.tensor_scalar(rsum[:, c + 1:c + 2], rsum[:, c + 1:c + 2], lamt[:, 5:6], None,
                                                  ALU.mult))
                    nc.vector.scalar_tensor_tensor(out=p1, in0=p1, scalar=rsum[:, c + 1:c + 2], in1=p0,
                                                   op0=ALU.mult, op1=ALU.add).then_inc(mix_ready, 1)
                else:
                    if u == N_DIFF:
                        row_max(t, u + N_DIFF)
                    if u + 1 < 12:
                        row_max(t, u + 1 + N_DIFF)
                n = 12 * t + u
                dve.wait_ge(PT_ready, n + 1)
                if n >= 2:
                    dve.wait_ge(pv_done, n - 1)
                nc.vector.tensor_copy(PT[u % 2][0:N_META, SEQ:SEQ + P],
                                      meta_T(2 * u + 1 if u < N_DIFF else u + N_DIFF)).then_inc(PTm_copied, 1)
                if u == N_DIFF:
                    dve.wait_ge(pv_done, 12 * t + N_DIFF)
                    nc.vector.tensor_copy(ya, OV[:, :]).then_inc(od_copied, 1)

            def heads_out(t, _):
                after(nc.vector.reciprocal(rsum[:, 8:16], psum_p[:, 8:16]))
                dve.wait_ge(pv_done, 12 * (t + 1))
                nc.vector.tensor_tensor(v3(yb), v3(OV[:, :]), rsum[:, 8:16].unsqueeze(2).to_broadcast([P, 8, DH]),
                                        ALU.mult).then_inc(yb_ready, 1)
                wait_squares()
                after(nc.vector.tensor_reduce(ss[:, 0:4], ysq.rearrange("p (h d) -> p h d", h=4), AX.X, ALU.add))
                inverse_root(P, 4, DV)
                y3 = ya.rearrange("p (h d) -> p h d", h=4)
                nc.vector.tensor_tensor(y3, y3, rstd[:, 0:4].unsqueeze(2).to_broadcast([P, 4, DV]),
                                        ALU.mult).then_inc(ya_ready, 1)

            def yT_(t, b):
                dve.wait_ge(yT_psum, 2 * t + b + 1)
                dst = yT[:, b, :, :].rearrange("p k q -> p (k q)")
                if b == 0:
                    nc.vector.tensor_scalar(dst, TR[:, :], small[:, K_SUB:K_SUB + 1], 1.0 - LAMBDA_INIT,
                                            ALU.mult, ALU.mult).then_inc(yT_ready, 1)
                else:
                    nc.vector.tensor_copy(dst, TR[:, :]).then_inc(yT_ready, 1)

            def merge(t, _):
                for n in range(2):
                    dve.wait_ge(chunk_done, group_done(4, "branch", t, 2 + n))
                    nc.vector.scalar_tensor_tensor(out=tg[:, n, :], in0=tg[:, n, :], scalar=1.0, in1=bank(n),
                                                   op0=ALU.add, op1=ALU.mult)
                    after(nc.vector.scalar_tensor_tensor(out=tg[:, 2 + n, :], in0=tg[:, 2 + n, :], scalar=1.0,
                                                         in1=bank(2 + n), op0=ALU.add, op1=ALU.mult))
                    nc.vector.tensor_tensor(merged[:, n * W:(n + 1) * W], tg[:, n, :], tg[:, 2 + n, :],
                                            ALU.add).then_inc(merged_ready, 1)

            def out_(t, n):
                dve.wait_ge(chunk_done, group_done(KD, "out", t, n))
                if n == 0:
                    dve.wait_ge(x_in[hsb(t)], x_count(t))
                hb = hs[:, hsb(t), n * W:(n + 1) * W]
                nc.vector.scalar_tensor_tensor(out=hb, in0=bank(2 + n), scalar=0.5, in1=hb, op0=ALU.mult,
                                               op1=ALU.add).then_inc(hs_ready, 1)

            def h2_(t, _):
                wait_squares()
                inverse_root(P, 1, D)
                nc.vector.scalar_tensor_tensor(out=h2[:, hsb(t), :], in0=hs[:, hsb(t), :], scalar=rstd[:, 0:1],
                                               in1=ffng[:, :], op0=ALU.mult, op1=ALU.mult).then_inc(h2_ready, 1)

            def top16(vals, inds, src, n, signal=None, value=None):
                after(nc.vector.max(vals[:, 0:8], src))
                nc.vector.max_index(inds[:, 0:8], vals[:, 0:8], src)
                ins = nc.vector.match_replace(scrap[:, 0:n], vals[:, 0:8], src, LOWEST)
                if signal is not None:
                    ins.then_inc(signal, 1)
                    dve.wait_ge(signal, value)
                else:
                    after(ins)
                after(nc.vector.max(vals[:, 8:16], scrap[:, 0:n]))
                after(nc.vector.max_index(inds[:, 8:16], vals[:, 8:16], scrap[:, 0:n]))

            def keys(t, n):
                m = 4 * t + n
                dve.wait_ge(key_scores, m + 1)
                for j in range(4):
                    top16(top[:, 4 * n + j, :], topi[:, 4 * n + j, :], OV[:, j * P:(j + 1) * P], NKEYS,
                          keys_taken if j == 3 else None, m + 1)

            def route(t, n):
                m = 4 * t + n
                hh = slice(2 * n, 2 * n + 2)
                for h in (2 * n, 2 * n + 1):
                    after(nc.vector.tensor_tensor(cand.rearrange("p (a b) -> p a b", a=TOPK),
                                                  top[:, 2 * h, :].unsqueeze(2).to_broadcast([P, TOPK, TOPK]),
                                                  top[:, 2 * h + 1, :].unsqueeze(1).to_broadcast([P, TOPK, TOPK]),
                                                  ALU.add))
                    top16(best[:, h, :], posn[:, h, :], cand, TOPK * TOPK)
                e0 = n * 2 * TOPK
                g2 = gate[:, t % 2, e0:e0 + 2 * TOPK].rearrange("p (h k) -> p h k", h=2)
                nc.vector.tensor_tensor(g2, best[:, hh, :], best[:, hh, 0:1].to_broadcast([P, 2, TOPK]),
                                        ALU.subtract).then_inc(gate_shift, 1)
                nc.vector.tensor_copy(topf[:, 4 * n:4 * n + 4, :], topi[:, 4 * n:4 * n + 4, :])
                nc.vector.tensor_scalar(posa[:, 0, :, :], posn[:, hh, :], 4, None, ALU.logical_shift_right)
                after(nc.vector.tensor_scalar(posa[:, 1, :, :], posn[:, hh, :], TOPK - 1, None, ALU.bitwise_and))
                after(nc.vector.tensor_copy(work[:, 3648:3712], work[:, 3584:3648].bitcast(U32)))
                if m == 0:
                    dve.wait_ge(iota_ready, 1)
                for c in range(2):
                    for h in range(2):
                        ins = nc.vector.tensor_tensor(hot[:, h, :, :],
                                                      posf[:, c, h, :].unsqueeze(2).to_broadcast([P, TOPK, TOPK]),
                                                      iota16[:, :].unsqueeze(1).to_broadcast([P, TOPK, TOPK]),
                                                      ALU.is_equal)
                    after(ins)
                    for h in range(2):
                        ins = nc.vector.tensor_tensor(hot[:, h, :, :], hot[:, h, :, :],
                                                      topf[:, 4 * n + 2 * h + c, :].unsqueeze(1)
                                                      .to_broadcast([P, TOPK, TOPK]), ALU.mult)
                    after(ins)
                    after(nc.vector.tensor_reduce(sel[:, c, :, :].rearrange("p h k -> p (h k)"),
                                                  hot.rearrange("p h k a -> p (h k) a"), AX.X, ALU.add))
                dve.wait_ge(gate_exp, m + 1)
                after(nc.vector.tensor_reduce(gsum[:, 0, hh], g2, AX.X, ALU.add))
                after(nc.vector.reciprocal(gsum[:, 1, hh], gsum[:, 0, hh]))
                nc.vector.tensor_tensor(g2, g2, gsum[:, 1, hh].unsqueeze(2).to_broadcast([P, 2, TOPK]), ALU.mult)
                nc.vector.scalar_tensor_tensor(out=idx[:, t % 2, e0:e0 + 2 * TOPK],
                                               in0=sel[:, 0, :, :].rearrange("p h k -> p (h k)"),
                                               scalar=float(NKEYS), in1=sel[:, 1, :, :].rearrange("p h k -> p (h k)"),
                                               op0=ALU.mult, op1=ALU.add).then_inc(route_ready, 1)
                dve.wait_ge(route_ready, m + 1)

            def weigh(t, e):
                n, w = NE * t + e, e % (2 * RING)
                dve.wait_ge(act_ready, n // 2 + 1)
                nc.vector.tensor_tensor(wexp[:, w:w + 2], acts[:, w:w + 2], gate[:, t % 2, e:e + 2],
                                        ALU.mult).then_inc(wexp_ready, 1)
                for j in (e, e + 1):
                    if j % 4 not in V_ON_DVE:
                        continue
                    dve.wait_ge(wexp_ready, n // 2 + 1)
                    k = N_DVE * t + dve_count(j)
                    if k >= 1:
                        dve.wait_ge(row_used_dve, k)
                    hb = hs[:, hsb(t), :]
                    w = j % (2 * RING)
                    nc.vector.scalar_tensor_tensor(out=hb, in0=ring[:, j % RING, D:2 * D], scalar=wexp[:, w:w + 1],
                                                   in1=hb, op0=ALU.mult, op1=ALU.add).then_inc(row_used_dve, 1)

            def experts_(t, span):
                for e in range(*span):
                    n = NE * t + e
                    dve.wait_ge(row_landed[e % RING], 16 * (n // RING + 1))
                    u_row = ring[:, e % RING, 0:D]
                    w = e % (2 * RING)
                    nc.vector.tensor_tensor_reduce(out=u_row, in0=u_row, in1=h2[:, hsb(t), :], scale=1.0, scalar=0.0,
                                                   op0=ALU.mult, op1=ALU.add,
                                                   accum_out=dots[:, w:w + 1]).then_inc(dot_ready, 1)
                    if e % 2 == 1 and e > span[0] + 1:
                        weigh(t, e - 3)
                weigh(t, span[1] - 2)

            def finish(t, _):
                dve.wait_ge(row_used, N_PE * (t + 1))
                dve.wait_ge(row_used_dve, N_DVE * (t + 1))
                hb = hs[:, hsb(t), :]
                nc.vector.tensor_tensor(hb, hb, Y[:, :], ALU.add).then_inc(out_ready, 1)

            nc.vector.memset(ones[:, :], 1.0)
            nc.vector.memset(cum2[:, :, :], 0.0)
            after(nc.vector.memset(logf[:, :, :], 0.0))
            dve.wait_ge(consts_in, CONSTS)
            nc.vector.tensor_copy(mask_bf[:, :, :].rearrange("p b k -> p (b k)"), work[:, 2048:2048 + 2 * P])
            after(nc.vector.tensor_copy(ident_bf[:, :], ident[:, 0:P]))
            rw = work[:, 4096:4096 + R_W - D]
            qg, kg, lam = rw[:, 0:DH], rw[:, DH:2 * DH], rw[:, 2 * DH:2 * DH + 4 * DH]
            H = DH // 2
            for which, g in ((1, kg), (0, qg)):
                def gb(lo, hi):
                    return g[:, lo:hi].unsqueeze(1).to_broadcast([P, NKT, hi - lo])
                nc.vector.tensor_tensor(ropeC[:, which, :, :], ropeC[:, 0, :, :], gb(0, DH), ALU.mult)
                nc.vector.tensor_tensor(ropeS[:, which, :, 0:H], ropeS[:, 0, :, 0:H], gb(H, DH), ALU.mult)
                after(nc.vector.tensor_tensor(ropeS[:, which, :, H:DH], ropeS[:, 0, :, H:DH], gb(0, H), ALU.mult))
            for i in range(2):
                nc.vector.tensor_tensor_reduce(out=work[:, 5120:5120 + DH], in0=lam[:, 2 * i * DH:(2 * i + 1) * DH],
                                               in1=lam[:, (2 * i + 1) * DH:(2 * i + 2) * DH], scale=1.0, scalar=0.0,
                                               op0=ALU.mult, op1=ALU.add,
                                               accum_out=lamt[:, i:i + 1]).then_inc(lam_dots, 1)
                dve.wait_ge(lam_dots, i + 1)
            dve.wait_ge(lam_exp, 1)
            after(nc.vector.tensor_tensor(lamt[:, 4:5], lamt[:, 3:4], lamt[:, 2:3], ALU.subtract))
            nc.vector.tensor_scalar(lamt[:, 5:6], lamt[:, 4:5], -LAMBDA_INIT, None, ALU.add).then_inc(setup, 1)
            dve.wait_ge(setup, 1)

            def put_hT(i):
                c0, r = tiles[token_order[i]]
                dve.wait_ge(xT_ready, i + 1)
                src = SC[:, (i % 2) * D:(i % 2 + 1) * D].rearrange("p (k q) -> p k q", k=KD)[:, :, 0:r]
                nc.vector.tensor_tensor(hT[:, :, c0:c0 + r], src,
                                        small[:, K_MIXG:K_MIXG + KD].unsqueeze(2).to_broadcast([P, KD, r]),
                                        ALU.mult).then_inc(hT_ready, 1)

            for i, s in enumerate(token_order):
                r = tiles[s][1]
                wait_squares()
                inverse_root(r, 1, D)
                if i >= 2:
                    dve.wait_ge(xT_ready, i - 1)
                nc.vector.tensor_scalar(xn[i % 2][0:r, :], hs[0:r, i % 2, :], rstd[0:r, 0:1], None,
                                        ALU.mult).then_inc(xn_ready, 1)
                if i >= 1:
                    put_hT(i - 1)
            put_hT(NKT - 1)
            work_of = {"kv": kv, "kT": kT_, "forget": forget, "q": q, "qT": qT_, "unit": unit, "heads_out": heads_out,
                       "yT": yT_, "merge": merge, "out": out_, "h2": h2_, "keys": keys, "route": route,
                       "experts": experts_, "finish": finish}
            for k, t, a in order:
                if k in work_of:
                    work_of[k](t, a)

        @block.gpsimd
        def _(pool):
            nc.gpsimd.iota(iota16[:, :], pattern=[[1, TOPK]], base=0, channel_multiplier=0,
                           allow_small_or_imprecise_dtypes=True).then_inc(iota_ready, 1)
            for t in range(NT):
                for e in range(NE):
                    if e % (2 * TOPK) == 0:
                        pool.wait_ge(route_ready, 4 * t + e // (2 * TOPK) + 1)
                    n = NE * t + e
                    if n >= RING:
                        if e % 4 in V_ON_DVE:
                            pool.wait_ge(row_used_dve, dve_count(n - RING) + 1)
                        else:
                            pool.wait_ge(row_used, pe_count(n - RING) + 1)
                    pool.indirect_dma_start(ring[:, e % RING, :], None, experts[:, :],
                                            bass.IndirectOffsetOnAxis(ap=idx[:, t % 2, e:e + 1], axis=0)
                                            ).then_inc(row_landed[e % RING], 16)


def kernel(**inputs):
    import numpy as np
    import concourse.bacc as bacc
    from concourse.bass_utils import run_bass_kernel_spmd

    nc = bacc.Bacc("TRN2", target_bir_lowering=False, num_devices=1)

    def flat(name):
        return np.ascontiguousarray(np.asarray(inputs[name])[0])

    tri = (np.arange(P)[:, None] <= np.arange(P)[None, :]).astype(np.float32)
    col = np.arange(P)[None, :]
    row = np.arange(P)[:, None]
    mask_f = np.where(col <= row, 0.0, MASKED)
    mask_d = np.where(col // CHUNK <= row // CHUNK, 0.0, MASKED)
    table = np.concatenate([np.eye(P), tri, mask_d, mask_f], axis=1).astype(np.float32)
    pos = np.concatenate([np.arange(SEQ) + N_META, np.arange(N_META), np.zeros(P - N_META)]).astype(np.float32)
    inv = np.float32(ROPE_THETA) ** (-np.arange(0, DH, 2, dtype=np.float32) / np.float32(DH))
    ang = pos[:, None] * inv[None, :].astype(np.float32)
    cos, sin = np.cos(ang), np.sin(ang)
    rope = np.concatenate([cos, cos, -sin, sin], axis=1).astype(np.float32)
    rope = np.ascontiguousarray(rope.reshape(NT + 1, P, 2 * DH).transpose(1, 0, 2))
    r = np.arange(P)
    lower = ((r >= 8) & (r < 16)).astype(np.float32)
    head = np.arange(N_FOX)[None, :]
    lsel = (r[:, None] == head).astype(np.float32)
    lneg = -(r[:, None] - 8 == head).astype(np.float32)

    two = lambda a: np.concatenate([a, a])[:, None]
    cols = np.concatenate([flat("norm_mix_g").reshape(KD, P).T, two(flat("fox_qnorm_g")), two(flat("fox_knorm_g")),
                           flat("diff_subln_g")[:, None], lower[:, None], 1.0 - lower[:, None], lsel, lneg],
                          axis=1).astype(np.float32)
    rows = np.concatenate([flat("norm_ffn_g"), flat("diff_qnorm_g"), flat("diff_knorm_g"),
                           flat("diff_lambda").reshape(-1)])
    arrays = {
        "x": np.ascontiguousarray(np.asarray(inputs["x"])[0]),
        "meta": np.ascontiguousarray(inputs["meta_tokens"]),
        "w_in": flat("w_in"), "b_gate": np.ascontiguousarray(inputs["b_gate"]),
        "b_forget": np.ascontiguousarray(inputs["b_forget"]),
        "w_bd": flat("w_branch_diff"), "w_bf": flat("w_branch_fox"), "w_out": flat("w_out"),
        "w_pq": flat("peer_w_q"),
        "subkeys_t": np.ascontiguousarray(flat("peer_subkeys").transpose(3, 0, 1, 2).reshape(P, 2 * PH, NKEYS)),
        "experts": np.concatenate([flat("peer_u"), flat("peer_v")], axis=1),
        "table": table, "cols": cols, "rows": np.tile(rows[None, :], (P, 1)), "rope": rope,
    }
    aps = {n: nc.dram_tensor(n, a.shape, mybir.dt.from_np(a.dtype), kind="ExternalInput").ap()
           for n, a in arrays.items()}
    out = nc.dram_tensor("out", (SEQ, D), F32, kind="ExternalOutput").ap()
    build(nc, **aps, out=out)
    res = run_bass_kernel_spmd(nc, [arrays], core_ids=[0])
    return res.results[0]["out"].reshape(1, SEQ, D)
```

```python
from contextlib import ExitStack

import concourse.bass as bass
from concourse import mybir

ALU = mybir.AluOpType
ACT = mybir.ActivationFunctionType
AX = mybir.AxisListType
F32 = mybir.dt.float32
F32R = mybir.dt.float32r
BF16 = mybir.dt.bfloat16
U32 = mybir.dt.uint32

P = 128
D = 1024
KD = D // P
SEQ = 512
N_META = 16
NT = SEQ // P
KEYS = SEQ + N_META
CHUNK = 64
EPS = 1e-6
LAMBDA_INIT = 0.2
ROPE_THETA = 10000.0

DH, DV, DPAIRS = 64, 128, 4
N_DIFF, N_FOX = 4, 8
W = 512
DQ, DK, DVO, FQ, FK, FV = (i * W for i in range(6))
FF = 6 * W
GATES = FF + N_FOX

PH, NKEYS, TOPK = 8, 128, 16
SLOTS = PH * TOPK
WSLOTS = 4
WK = 2
GT = 32
GBLK = SEQ // GT
G4 = 4
HOTS = 3
POOLS = 2
AHEAD = 2
EB = 4
NB = NKEYS // EB
FILL = 2
MAPS = 1
EARLY = 6
LOWEST = -3.0e38
MASKED = -1.0e30

C_ID, C_TRI, C_MASKD, C_MASKF, C_W = 0, P, 2 * P, 3 * P, 4 * P
K_MIXG, K_FQG, K_FKG, K_SUB, K_ROW0, K_ROW1, K_LSEL, K_LNEG, K_FFNG = 0, 8, 9, 10, 11, 12, 13, 21, 29
K_W = 37
R_QG, R_KG, R_LAM, R_W = 0, DH, 2 * DH, 6 * DH


def build(nc, x, meta, w_in, b_gate, b_forget, w_bd, w_bf, w_out, w_pq, subkeys_t, u_t, v,
          table, cols, rows, rope, gate_map, out):
    with ExitStack() as ctx:
        def sb(name, shape, dt=F32):
            return ctx.enter_context(nc.sbuf_tensor(name, shape, dt))

        def sem(name):
            return ctx.enter_context(nc.semaphore(name))

        h2T_at, ARENA = 40064, 40064 + KD * SEQ
        arena = sb("arena", [P, ARENA])
        base = nc.sbuf_base - 4 * ARENA
        spans = {}

        def carve(names, at=0):
            for name, n in names:
                spans[name] = arena[:, at:at + n]
                at += n
            assert at <= h2T_at

        def over(name, at, dims, dt=F32):
            return nc.alloc_sbuf_tensor_at(name, [P, *dims], dt, offset=base + 4 * at)[:]

        carve((("kT", 2 * DPAIRS * KEYS), ("V", 2 * (NT + 1) * W), ("hT", KD * KEYS), ("wring", WSLOTS * WK * W),
               ("subk", 2 * PH * NKEYS), ("work", 6144), ("choice", 2944),
               ("onehot", HOTS * G4 * 2 * P), ("gbuf", 2 * NKEYS * GT)))
        kT = spans["kT"].rearrange("p (b j k) -> p b j k", b=2, j=DPAIRS)
        V = spans["V"].rearrange("p (b s w) -> p b s w", b=2, s=NT + 1)
        hT = spans["hT"].rearrange("p (k q) -> p k q", k=KD)
        wring = spans["wring"].rearrange("p (s k w) -> p s k w", s=WSLOTS, k=WK)
        wring_T = spans["wring"].rearrange("p (s k w) -> p s k w", s=WSLOTS, k=KD)
        subk = spans["subk"].rearrange("p (n k) -> p n k", n=2 * PH)
        choice = spans["choice"]
        work = spans["work"]
        gbuf = spans["gbuf"].rearrange("p (b e t) -> p b e t", b=2, e=NKEYS)
        onehot = spans["onehot"].rearrange("p (b x c k) -> p b x c k", b=HOTS, x=G4, c=2)
        at = {}
        end = 0
        for name, n in (("u", EB * D), ("h_hi", KD * SEQ), ("h_lo", KD * SEQ), ("w0", EB * SEQ), ("w_hi0", EB * SEQ),
                        ("w1", EB * SEQ), ("w_hi1", EB * SEQ), ("u_hi", EB * D), ("v0", EB * W), ("v_hi0", EB * W), ("v1", EB * W),
                        ("v_hi1", EB * W), ("g0", EB * SEQ), ("g1", EB * SEQ)):
            at[name] = end
            end += n
        assert end <= h2T_at
        u_whole = over("u_whole", at["u"], [EB, KD, P])
        u_lo = over("u_lo", at["u"], [EB, KD, P], F32R)
        u_hi = over("u_hi", at["u_hi"], [EB, KD, P], F32R)
        h_hi = over("h_hi", at["h_hi"], [KD, SEQ], F32R)
        h_lo = over("h_lo", at["h_lo"], [KD, SEQ], F32R)
        w_whole = [over(f"w_whole{i}", at[f"w{i}"], [EB, SEQ]) for i in range(2)]
        w_lo = [over(f"w_lo{i}", at[f"w{i}"], [EB, SEQ], F32R) for i in range(2)]
        w_hi = [over(f"w_hi{i}", at[f"w_hi{i}"], [EB, SEQ], F32R) for i in range(2)]
        v_whole = [over(f"v_whole{i}", at[f"v{i}"], [EB, W]) for i in range(2)]
        v_lo = [over(f"v_lo{i}", at[f"v{i}"], [EB, W], F32R) for i in range(2)]
        v_hi = [over(f"v_hi{i}", at[f"v_hi{i}"], [EB, W], F32R) for i in range(2)]
        gates = [over(f"gates{i}", at[f"g{i}"], [GBLK, EB, GT]) for i in range(2)]
        h2T = arena[:, h2T_at:h2T_at + KD * SEQ].rearrange("p (k q) -> p k q", k=KD)
        hs = sb("hs", [P, NT, D])
        ropeC = sb("ropeC", [P, 2, NT + 1, DH])
        ropeS = sb("ropeS", [P, 2, NT + 1, DH])
        ident = sb("ident", [P, 2 * P])
        ident_bf = sb("ident_bf", [P, P], BF16)
        mask_bf = sb("mask_bf", [P, 2, P], BF16)
        small = sb("small", [P, K_W])
        ones = sb("ones", [P, P])
        bgate = sb("bgate", [P, W])
        wf = sb("wf", [P, KD, N_FOX])
        bf = sb("bf", [1, N_FOX])
        logf = sb("logf", [P, NT + 1, N_FOX])
        cum2 = sb("cum2", [P, NT + 1, 2 * N_FOX])
        decR = sb("decR", [16, KEYS])
        cumT = sb("cumT", [16, SEQ])
        lamt = sb("lamt", [P, 8])
        ss = sb("ss", [P, 8])
        std = sb("std", [P, 8])
        rstd = sb("rstd", [P, 8])
        nmax = sb("nmax", [P, 16])
        psum_p = sb("psum_p", [P, 16])
        rsum = sb("rsum", [P, 16])
        sel = sb("sel", [P, 2, SLOTS])
        gate = sb("gate", [P, SLOTS])
        slot = sb("slot", [P, 3, P])
        iota16 = sb("iota16", [P, TOPK])
        iota128 = sb("iota128", [P, NKEYS])
        gsum = sb("gsum", [P, 2, PH])

        v_t = v.rearrange("(b j p) n -> b p j n", j=EB, p=P)
        gate_map_t = gate_map.rearrange("b p (n e) t -> n p b (e t)", e=EB)

        xin = [gbuf[:, i, :, :].rearrange("p e t -> p (e t)")[:, 0:D] for i in range(2)]
        xn = [gbuf[:, i, :, :].rearrange("p e t -> p (e t)")[:, 2 * D:3 * D] for i in range(2)]
        xsq = gbuf[:, 0, :, :].rearrange("p e t -> p (e t)")[:, D:2 * D]
        heads = [work[:, 0:W], work[:, 5120:5120 + W]]
        qT = [work[:, 512:1024].rearrange("p (j q) -> p j q", j=DPAIRS),
              work[:, 1024:1536].rearrange("p (j q) -> p j q", j=DPAIRS)]
        qraw = work[:, 1536:2048]
        qA = work[:, 2048:2560]
        probs = [work[:, 1536 + i * KEYS:1536 + (i + 1) * KEYS] for i in range(4)]
        PT = [work[:, 3648 + i * 640:3648 + (i + 1) * 640] for i in range(2)]
        ya, yb = work[:, 5120:5632], work[:, 5632:6144]
        ysq = work[:, 0:W]
        tg = work[:, 0:2048].rearrange("p (n w) -> p n w", n=4)
        merged = work[:, 2048:3072]
        mT = work[:, 3072:4096].rearrange("p (k q) -> p k q", k=KD)
        yT = work[:, 4096:5120].rearrange("p (b k q) -> p b k q", b=2, k=4)
        hsq = work[:, 5120:6144]
        h2 = work[:, 0:1024]
        pqT = choice[:, 0:1024].rearrange("p (b j q) -> p b j q", b=2, j=4)
        scrap = choice[:, 1024:1280]
        cand = choice[:, 1280:1536]
        hot = choice[:, 1280:1792].rearrange("p (h k a) -> p h k a", h=2, k=TOPK)

        decL = [work[0:16, 0:W].rearrange("p (h q) -> p h q", h=4),
                work[0:16, 5632:5632 + W].rearrange("p (h q) -> p h q", h=4)]

        def routing(at, dt, *dims):
            n = 1
            for d in dims:
                n *= d
            v = choice[:, at:at + n] if dt is F32 else choice[:, at:at + n].bitcast(dt)
            names = "abc"[:len(dims)]
            return v.rearrange(f"p ({' '.join(names)}) -> p {' '.join(names)}", **dict(zip(names, dims)))

        top = routing(1920, F32, 2 * PH, TOPK)
        topi = routing(2176, U32, 2 * PH, TOPK)
        topf = routing(2432, F32, 2 * PH, TOPK)
        best = routing(2688, F32, PH, TOPK)
        posn = routing(2816, U32, PH, TOPK)
        posa = routing(1792, U32, 2, 2, TOPK)
        posf = routing(1856, F32, 2, 2, TOPK)

        SC = ctx.enter_context(nc.psum_tensor("SC", [P, 4 * W], F32))
        TR = ctx.enter_context(nc.psum_tensor("TR", [P, W], F32))
        OV = ctx.enter_context(nc.psum_tensor("OV", [P, W], F32))
        Y = ctx.enter_context(nc.psum_tensor("Y", [P, D], F32))

        def bank(i):
            return SC[:, i * W:(i + 1) * W]

        def part_bank(o):
            return (TR[:, :], OV[:, :], Y[:, 0:W], Y[:, W:2 * W])[o % 4]

        def meta_T(c):
            b = (c % 2) * 2 * W
            return SC[0:N_META, b + 640:b + 640 + P]

        early_in = sem("early_in")
        consts_in = sem("consts_in")
        x_in = [sem("x_in0"), sem("x_in1")]
        res_in = sem("res_in")
        w_in_sem = [sem(f"w_landed{i}") for i in range(WSLOTS)]
        chunk_done = sem("chunk_done")
        dve_step = sem("dve_step")
        act_step = sem("act_step")
        setup = sem("setup")
        iota_ready = sem("iota_ready")
        sq_ready = sem("sq_ready")
        var_ready = sem("var_ready")
        std_ready = sem("std_ready")
        xn_ready = sem("xn_ready")
        xT_ready = sem("xT_ready")
        hT_ready = sem("hT_ready")
        kv_ready = sem("kv_ready")
        heads_ready = sem("heads_ready")
        headsT_ready = sem("headsT_ready")
        qk_ready = sem("qk_ready")
        v_copied = sem("v_copied")
        f_ready = sem("f_ready")
        f_neg = sem("f_neg")
        f_soft = sem("f_soft")
        logf_ready = sem("logf_ready")
        cum_ready = sem("cum_ready")
        cum_copied = sem("cum_copied")
        cumT_ready = sem("cumT_ready")
        dec_ready = sem("dec_ready")
        lam_dots = sem("lam_dots")
        lam_exp = sem("lam_exp")
        scores_ready = sem("scores_ready")
        max_ready = sem("max_ready")
        exp_ready = sem("exp_ready")
        mix_ready = sem("mix_ready")
        PT_ready = sem("PT_ready")
        PT_copied = sem("PT_copied")
        PTm_copied = sem("PTm_copied")
        pv_done = sem("pv_done")
        od_copied = sem("od_copied")
        yb_ready = sem("yb_ready")
        ya_ready = sem("ya_ready")
        yT_psum = sem("yT_psum")
        yT_ready = sem("yT_ready")
        tanh_ready = sem("tanh_ready")
        merged_ready = sem("merged_ready")
        mT_psum = sem("mT_psum")
        mT_ready = sem("mT_ready")
        hs_ready = sem("hs_ready")
        h2_ready = sem("h2_ready")
        h2T_psum = sem("h2T_psum")
        h2T_ready = sem("h2T_ready")
        pqT_copied = sem("pqT_copied")
        key_scores = sem("key_scores")
        keys_taken = sem("keys_taken")
        gate_shift = sem("gate_shift")
        gate_exp = sem("gate_exp")
        route_ready = sem("route_ready")
        slot_psum = sem("slot_psum")
        slot_ready = sem("slot_ready")
        hot1_ready = sem("hot1_ready")
        hot2_ready = sem("hot2_ready")
        gmap_psum = sem("gmap_psum")
        gmap_copied = sem("gmap_copied")
        gmap_stored = [sem(f"gmap_stored{i}") for i in range(2)]
        h_high = sem("h_high")
        h_split = sem("h_split")
        u_landed = [sem(f"u_landed{i}") for i in range(EB)]
        u_high = sem("u_high")
        u_split = sem("u_split")
        v_landed = [sem(f"v_landed{i}") for i in range(2)]
        v_high = sem("v_high")
        v_split = sem("v_split")
        g_landed = [sem(f"g_landed{i}") for i in range(2)]
        pre_ready = sem("pre_ready")
        act_ready = sem("act_ready")
        w_gated = sem("w_gated")
        w_high = sem("w_high")
        w_split = sem("w_split")
        part_ready = sem("part_ready")
        part_added = sem("part_added")
        out_stored = sem("out_stored")

        N_CONST = 10
        KV = [DK, FK, DVO, FV]
        tiles = [(s * P, P) for s in range(NT)] + [(SEQ, N_META)]
        NKT = len(tiles)

        PASSES = [(NT, 0), (1, 2, 3)]
        front = ([("q", 0), ("q", 1), ("qT", 0), ("qT", 1)]
                 + [(k, u) for u in range(12) for k in ("maps", "unit")] + [("heads_out", 0)]
                 + [("gate", n) for n in range(4)] + [("yT", 0), ("yT", 1)]
                 + [("branch", n) for n in range(4)] + [("merge", 0), ("out", 0), ("out", 1), ("h2", 0), ("h2T", 0)])
        choose = [("pq", 0)]
        for n in range(4):
            choose += ([("pq", n + 1)] if n < 3 else []) + [("keys", n)] + [("top", (n, j)) for j in range(1, 4)]
            choose += [(k, (n, i)) for k in ("pairs", "numbers") for i in range(2)]
        cost = {"kv": 44.8, "kT": 4, "forget": 8, "q": 4.8, "qT": 3.75, "maps": 1.5, "unit": 3.2,
                "heads_out": 5, "gate": 7, "yT": 1.6, "branch": 3.2, "merge": 10, "out": 4.9, "h2": 5.0,
                "h2T": 1.2, "pq": 7, "keys": 2.8, "top": 1.5, "pairs": 0.84, "numbers": 2.5, "dense": 5,
                "slots": 2, "gmap": 1.2}

        def kv_pieces(p):
            return [("kv", (p, 0)), ("kT", (p, 0)), ("kv", (p, 1)), ("kT", (p, 1)), ("kv", (p, 2)), ("kv", (p, 3)),
                    ("forget", p)]

        def choice_and_front(t):
            groups, last = P // G4, []
            side = [(k, t, a) for k, a in choose] + [("slots", t, 0)]
            if t + 1 < NT:
                side += [("gmap", t, (m, m + 1)) for m in range(groups)]
                pieces = [(k, t + 1, a) for k, a in (kv_pieces(1) if t == 0 else []) + front]
            else:
                done = side.index(("pq", t, 3)) + 1
                early = [("dense", t, j) for j in range(2 * EB - FILL - MAPS)]
                order, rest = side[:1] + [("split", t, 0)] + side[1:done], side[done:]
                block0 = rest.index(("keys", t, 3)) + 1
                for n, piece in enumerate(rest):
                    if early and (early[0][2] < EB or n >= block0):
                        order.append(early.pop(0))
                    order.append(piece)
                side = [("gmap", t, (m, m + 1)) for m in range(groups)]
                pieces = [("dense", t, j) for j in range(2 * EB - FILL - MAPS, 2 * EB - FILL)]
                last = [("dense", t, j) for j in range(2 * EB - FILL, 2 * EB)]
            spread = sum(cost[k] for k, _, _ in side) / sum(cost[k] for k, _, _ in pieces)
            order, due = ([] if t + 1 < NT else order), 0
            for piece in pieces:
                order.append(piece)
                due += spread * cost[piece[0]]
                while side and due >= cost[side[0][0]] / 2:
                    due -= cost[side[0][0]]
                    order.append(side.pop(0))
            return order + side + last

        start = {}
        for i, at_ in ((2, 0), (3, 2), (4, 4)):
            start[at_] = start.get(at_, []) + [("norm", i)]
            start[at_ + 2] = start.get(at_ + 2, []) + [("normT", i)]
        first = [p for n, piece in enumerate(kv_pieces(0)) for p in [piece] + start.get(n, [])]
        order = [(k, 0, a) for k, a in first + front]
        for t in range(NT):
            order += choice_and_front(t)

        pe_order, held = [], []
        for piece in order:
            if piece[0] == "kT":
                held.append(piece)
                continue
            pe_order.append(piece)
            if piece[0] == "kv":
                pe_order += held
                held = []

        all_chunks, first_chunk = [], {}

        def add_group(key, w, c0, k_tiles):
            v = w.rearrange("(k p) n -> p k n", p=P)
            first_chunk[key] = len(all_chunks)
            all_chunks.extend(v[:, k:k + WK, c0:c0 + W] for k in range(0, k_tiles, WK))

        for k, t, a in order:
            if k == "kv":
                add_group((k, a), w_in, KV[a[1]], KD)
            elif k == "q":
                add_group((k, t, a), w_in, (DQ, FQ)[a], KD)
            elif k == "gate":
                add_group((k, t, a), w_in, GATES + a * W, KD)
            elif k == "branch":
                add_group((k, t, a), (w_bd, w_bf)[a // 2], (a % 2) * W, 4)
            elif k == "out":
                add_group((k, t, a), w_out, a * W, KD)
            elif k == "pq":
                first_chunk[k, t, a] = len(all_chunks)
                cols_pq = w_pq.rearrange("(k p) n -> p k n", p=P)
                all_chunks.extend(cols_pq[:, :, a * W + j * P:a * W + (j + 1) * P] for j in range(W // P))

        def group_done(k_tiles, *key):
            return first_chunk[key] + k_tiles // WK

        def kv_item(p, g, i):
            return (0 if p == 0 else 4 * len(PASSES[0])) + g * len(PASSES[p]) + i

        def kv_bank(p, g, i):
            return kv_item(p, g, i) % 4

        head_items = []
        for k, t, a in order:
            if k == "kv" and a[1] < 2:
                head_items += [("k", a[0], a[1], i) for i in range(len(PASSES[a[0]]))]
            elif k == "q":
                head_items.append(("q", t, a))
        head_no = {key: n for n, key in enumerate(head_items)}
        V_ITEMS = [0, 2 * len(PASSES[0])]

        def wait_kv(eng, p, g, i):
            if i < len(PASSES[p]) - 1:
                before = 0 if p == 0 else 4 * (len(PASSES[0]) - 1)
                eng.wait_ge(kv_ready, before + g * (len(PASSES[p]) - 1) + i + 1)
            else:
                eng.wait_ge(chunk_done, group_done(KD, "kv", (p, g)))

        N_LOADS = 11
        CONSTS = 16 * N_LOADS
        N_GROUPS = SEQ // G4

        token_order = [NT, 0, 1, 2, 3]
        block = ctx.enter_context(nc.Block())

        @block.sync
        def _(sp):
            def load_x(i, t):
                c0, r = tiles[t]
                src = x[c0:c0 + r, :] if t < NT else meta
                sp.dma_start(xin[i % 2][0:r, :], src).then_inc(x_in[i % 2], 16)

            def load_chunk(n):
                if n >= WSLOTS:
                    sp.wait_ge(chunk_done, n - WSLOTS + 1)
                dst = (wring if all_chunks[n].shape[1] == WK else wring_T)[:, n % WSLOTS, :, :]
                sp.dma_start(dst, all_chunks[n]).then_inc(w_in_sem[n % WSLOTS], 16)

            load_x(0, token_order[0])
            load_x(1, token_order[1])
            sp.dma_start(small[:, :], cols).then_inc(early_in, 16)
            sp.dma_start(ident[:, :], table[:, 0:2 * P]).then_inc(early_in, 16)
            consts = [(work[:, 2048:2048 + 2 * P], table[:, 2 * P:C_W]),
                      (ropeC[:, 0, :, :], rope[:, :, 0:DH]), (ropeS[:, 0, :, :], rope[:, :, DH:2 * DH]),
                      (work[:, 4096:4096 + R_W], rows),
                      (subk[:, :, :], subkeys_t),
                      (wf[:, :, :], w_in[:, FF:FF + N_FOX].rearrange("(k p) n -> p k n", p=P)),
                      (bf[:, :], b_forget)]
            consts += [(bgate[32 * n:32 * n + 1, :], b_gate[:, n * W:(n + 1) * W]) for n in range(4)]
            assert len(consts) == N_LOADS
            for n in range(2):
                load_chunk(n)
            for dst, src in consts:
                sp.dma_start(dst, src).then_inc(consts_in, 16)
            for n in range(2, WSLOTS):
                load_chunk(n)
            for i in range(2, NKT):
                if i == 4:
                    for n in range(WSLOTS, 2 * WSLOTS):
                        load_chunk(n)
                sp.wait_ge(xn_ready, i - 1)
                load_x(i, token_order[i])
            for t in range(NT):
                sp.dma_start(hs[:, t, :], x[t * P:(t + 1) * P, :]).then_inc(res_in, 16)
            def load_u(b, j):
                if not (isinstance(b, int) and b == 0):
                    sp.wait_ge(pre_ready, b * EB + (j + 1 - EB))
                sp.dma_start(u_whole[:, j, :, :], u_t[b * EB + j]).then_inc(u_landed[j], 16)

            def load_v(b, h):
                if not (isinstance(b, int) and b == 0):
                    sp.wait_ge(part_ready, b * (2 * NT) + (NT * (h + 1) - 2 * NT))
                sp.dma_start(v_whole[h], v_t[b][:, :, h * W:(h + 1) * W]).then_inc(v_landed[h], 16)

            def load_g(b, parity):
                if not (isinstance(b, int) and b < 2):
                    sp.wait_ge(w_gated, b * EB - EB)
                sp.dma_start(gates[parity].rearrange("p b j t -> p b (j t)"), gate_map_t[b]).then_inc(g_landed[parity], 16)

            def loads(b, parity, last=False):
                if not last:
                    load_g(b + 1, (parity + 1) % 2)
                    load_u(b + 1, 0)
                    load_u(b + 1, 1)
                load_v(b, 0)
                if not last:
                    load_u(b + 1, 2)
                    load_u(b + 1, 3)
                load_v(b, 1)

            for n in range(2 * WSLOTS, len(all_chunks)):
                if n == first_chunk["pq", NT - 1, 1]:
                    sp.wait_ge(chunk_done, group_done(KD, "gate", NT - 1, 3))
                    for j in range(EB):
                        load_u(0, j)
                load_chunk(n)
            for j in range(EB):
                load_u(1, j)
            sp.wait_ge(slot_ready, NT)
            load_v(0, 0)
            load_u(2, 0)
            load_u(2, 1)
            for i in range(2):
                sp.wait_ge(gmap_stored[i], 16 * (GBLK // 2))
            load_g(0, 0)
            load_g(1, 1)
            load_v(0, 1)
            load_u(2, 2)
            load_u(2, 3)
            load_g(2, 0)
            load_v(1, 0)
            load_v(1, 1)
            with sp.Fori(1, NB // 2 - 1) as c:
                loads(c * 2, 0)
                loads(c * 2 + 1, 1)
            loads(NB - 2, 0)
            loads(NB - 1, 1, last=True)
            for t in range(NT):
                sp.wait_ge(part_added, 2 * NT * NB - NT + t + 1)
                sp.dma_start(out[t * P:(t + 1) * P, :], hs[:, t, :]).then_inc(out_stored, 16)
            sp.wait_ge(out_stored, 16 * NT)

        @block.tensor
        def _(pe):
            idm = ident[:, 0:P]
            tri = ident[:, P:2 * P]

            def use_chunks(key, k_tiles, lhs, acc, bias=None):
                if bias is not None:
                    nc.tensor.matmul(acc, *bias, start=True, stop=False)
                for j in range(k_tiles // WK):
                    n = first_chunk[key] + j
                    pe.wait_ge(w_in_sem[n % WSLOTS], 16 * (n // WSLOTS + 1))
                    for i in range(WK):
                        k = j * WK + i
                        mm = nc.tensor.matmul(acc, lhs(k), wring[:, n % WSLOTS, i, :],
                                              start=(k == 0 and bias is None), stop=(k == k_tiles - 1))
                    mm.then_inc(chunk_done, 1)

            def turn(dst, src, r=P):
                for j in range(src.shape[-1] // P):
                    mm = nc.tensor.transpose(dst[:, j * P:j * P + r], src[0:r, j * P:(j + 1) * P], ident[0:r, 0:r])
                return mm

            def headsT(key, r):
                i = head_no[key]
                if i == 0:
                    pe.wait_ge(setup, 1)
                pe.wait_ge(heads_ready, i + 1)
                if i >= 1:
                    pe.wait_ge(qk_ready, i)
                turn(TR, heads[i % 2], r).then_inc(headsT_ready, 1)

            def kv(t, a):
                p, g = a
                key_tiles = PASSES[p]
                if (p, g) == (1, 0):
                    pe.wait_ge(hT_ready, NKT)
                    pe.wait_ge(h2T_ready, 1)
                for j in range(KD // WK):
                    n = first_chunk[("kv", a)] + j
                    pe.wait_ge(w_in_sem[n % WSLOTS], 16 * (n // WSLOTS + 1))
                    for i, s in enumerate(key_tiles):
                        c0, r = tiles[s]
                        m = kv_item(p, g, i)
                        first = kv_item(p, 0, 0)
                        if j == 0 and m - 4 >= first:
                            g4, i4 = divmod(m - 4 - first, len(key_tiles))
                            if g4 < 2:
                                pe.wait_ge(heads_ready, head_no[("k", p, g4, i4)] + 1)
                            else:
                                pe.wait_ge(v_copied, V_ITEMS[p] + (g4 - 2) * len(key_tiles) + i4 + 1)
                        for b in range(WK):
                            k = j * WK + b
                            mm = nc.tensor.matmul(bank(m % 4)[0:r, :], hT[:, k, c0:c0 + r],
                                                  wring[:, n % WSLOTS, b, :], start=(k == 0), stop=(k == KD - 1))
                        if i == len(key_tiles) - 1:
                            mm.then_inc(chunk_done, 1)
                        elif j == KD // WK - 1:
                            mm.then_inc(kv_ready, 1)

            def kT_(t, a):
                p, g = a
                for i, s in enumerate(PASSES[p]):
                    headsT(("k", p, g, i), tiles[s][1])

            def forget(t, p):
                pe.wait_ge(qk_ready, head_no[("k", p, 1, len(PASSES[p]) - 1)] + 1)
                for s in PASSES[p]:
                    c0, r = tiles[s]
                    o = TR[0:r, s * N_FOX:(s + 1) * N_FOX]
                    nc.tensor.matmul(o, ones[0:1, 0:r], bf[:, :], start=True, stop=False)
                    for k in range(KD):
                        mm = nc.tensor.matmul(o, hT[:, k, c0:c0 + r], wf[:, k, :], start=False, stop=(k == KD - 1))
                mm.then_inc(f_ready, 1)
                pe.wait_ge(logf_ready, p + 1)
                for s in PASSES[p]:
                    r = tiles[s][1]
                    o = TR[0:r, s * N_FOX:(s + 1) * N_FOX]
                    if s == NT:
                        mm = nc.tensor.matmul(o, tri[0:N_META, 0:N_META], logf[0:N_META, NT, :], start=True, stop=True)
                        continue
                    nc.tensor.matmul(o, ones[0:N_META, :], logf[0:N_META, NT, :], start=True, stop=False)
                    for b in range(s):
                        nc.tensor.matmul(o, ones[:, :], logf[:, b, :], start=False, stop=False)
                    mm = nc.tensor.matmul(o, tri, logf[:, s, :], start=False, stop=True)
                mm.then_inc(cum_ready, 1)
                pe.wait_ge(cum_copied, p + 1)
                for i, s in enumerate(PASSES[p]):
                    r = tiles[s][1]
                    mm = nc.tensor.transpose(TR[0:16, i * P:i * P + r], cum2[0:r, s, :], ident[0:r, 0:r])
                mm.then_inc(cumT_ready, 1)

            def q(t, g):
                if g == 0 and t < 2:
                    pe.wait_ge(v_copied, 2 * sum(len(x_) for x_ in PASSES[0:t + 1]))
                if g == 0 and t >= 2:
                    pe.wait_ge(h2T_ready, t)
                use_chunks(("q", t, g), KD, lambda k: hT[:, k, t * P:(t + 1) * P], bank(g))

            def qT_(t, g):
                headsT(("q", t, g), P)

            def scores(t, c):
                n, nk = 16 * t + c, (t + 1) * P
                if c >= 2:
                    pe.wait_ge(exp_ready, n - 1)
                if c >= 9 or (c % 2 == 1 and c >= 3):
                    pe.wait_ge(PTm_copied, 12 * t + (c - 5 if c >= 9 else (c - 1) // 2))
                fox = c >= 2 * N_DIFF
                g = c - 8 if fox else (c % 2) * N_DIFF + c // 2
                lo = DH * (g % 2)
                query = qT[fox][lo:lo + DH, g // 2, :]
                b = (c % 2) * 2 * W
                acc, accm = SC[:, b:b + nk], SC[:, b + nk:b + nk + N_META]
                nc.tensor.matmul(acc, query, kT[lo:lo + DH, int(fox), g // 2, 0:nk], start=True, stop=False)
                if fox:
                    nc.tensor.matmul(acc, decL[g // 4][:, g % 4, :], decR[:, 0:nk], start=False, stop=False)
                nc.tensor.matmul(acc[:, nk - P:nk], ident_bf[:, :], mask_bf[:, int(fox), :], start=False, stop=True)
                mm = nc.tensor.matmul(accm, query, kT[lo:lo + DH, int(fox), g // 2, SEQ:KEYS], start=True,
                                      stop=not fox)
                if fox:
                    mm = nc.tensor.matmul(accm, decL[g // 4][:, g % 4, :], decR[:, SEQ:KEYS], start=False, stop=True)
                mm.then_inc(scores_ready, 1)

            def probsT(t, u):
                c = 2 * u + 1 if u < N_DIFF else u + N_DIFF
                if u < N_DIFF:
                    pe.wait_ge(mix_ready, N_DIFF * t + u + 1)
                else:
                    pe.wait_ge(exp_ready, 16 * t + c + 1)
                if u >= 1:
                    pe.wait_ge(PT_copied, 12 * t + u)
                    pe.wait_ge(PTm_copied, 12 * t + u)
                pr, nk = probs[c % 4], (t + 1) * P
                turn(TR, pr[:, 0:nk])
                nc.tensor.transpose(meta_T(c), pr[:, nk:nk + N_META], idm).then_inc(PT_ready, 1)

            def pv(t, u):
                n = 12 * t + u
                pe.wait_ge(PT_copied, n + 1)
                pe.wait_ge(PTm_copied, n + 1)
                if u == N_DIFF:
                    pe.wait_ge(od_copied, t + 1)
                fox = u >= N_DIFF
                wv = DH if fox else DV
                h = u - N_DIFF if fox else u
                o = OV[:, h * wv:(h + 1) * wv]
                pt = PT[u % 2]
                for s in range(t + 1):
                    nc.tensor.matmul(o, pt[:, s * P:(s + 1) * P], V[:, int(fox), s, h * wv:(h + 1) * wv],
                                     start=(s == 0), stop=False)
                nc.tensor.matmul(o, pt[0:N_META, SEQ:SEQ + P], V[0:N_META, int(fox), NT, h * wv:(h + 1) * wv],
                                 start=False, stop=True).then_inc(pv_done, 1)

            def maps(t, u):
                if u == 0:
                    pe.wait_ge(qk_ready, head_no[("q", t, 1)] + 1)
                    pe.wait_ge(dec_ready, t + 1 + (2 if t else 1))
                if u < N_DIFF:
                    scores(t, 2 * u)
                    scores(t, 2 * u + 1)
                    if u >= 1:
                        pv(t, u - 1)
                    return
                if u == N_DIFF:
                    scores(t, u + N_DIFF)
                    pv(t, u - 1)
                if u + 1 < 12:
                    scores(t, u + 1 + N_DIFF)

            def unit(t, u):
                probsT(t, u)
                if u > N_DIFF:
                    pv(t, u - 1)

            def heads_out(t, _):
                pv(t, 11)

            def gate_(t, n):
                use_chunks(("gate", t, n), KD, lambda k: hT[:, k, t * P:(t + 1) * P], bank(n),
                           (ones[32 * n:32 * n + 1, :], bgate[32 * n:32 * n + 1, :]))

            def yT_(t, b):
                if b == 0:
                    pe.wait_ge(ya_ready, t + 1)
                else:
                    pe.wait_ge(yb_ready, t + 1)
                    pe.wait_ge(yT_ready, 2 * t + 1)
                turn(TR, (ya, yb)[b]).then_inc(yT_psum, 1)

            def branch(t, n):
                b = n // 2
                pe.wait_ge(yT_ready, 2 * t + b + 1)
                pe.wait_ge(tanh_ready, 4 * t + n + 1)
                use_chunks(("branch", t, n), 4, lambda k: yT[:, b, k, :], bank(n))

            def merge(t, _):
                pe.wait_ge(merged_ready, 2 * t + 2)
                turn(SC, merged).then_inc(mT_psum, 1)

            def out_(t, n):
                pe.wait_ge(mT_ready, t + 1)
                use_chunks(("out", t, n), KD, lambda k: mT[:, k, :], bank(2 + n))

            def h2T_(t, _):
                pe.wait_ge(h2_ready, t + 1)
                turn(SC, h2).then_inc(h2T_psum, 1)

            def pq_(t, n):
                m = 4 * t + n
                pe.wait_ge(h2T_ready, t + 1)
                if n >= 1:
                    pe.wait_ge(pqT_copied, m)
                elif t >= 1:
                    pe.wait_ge(gmap_copied, t * (P // G4))
                for j in range(W // P):
                    c = first_chunk["pq", t, n] + j
                    pe.wait_ge(w_in_sem[c % WSLOTS], 16 * (c // WSLOTS + 1))
                    for k in range(KD):
                        mm = nc.tensor.matmul(Y[:, j * P:(j + 1) * P], wring_T[:, c % WSLOTS, k, :],
                                              h2T[:, k, t * P:(t + 1) * P], start=(k == 0), stop=(k == KD - 1))
                    mm.then_inc(chunk_done, 1)

            def keys(t, n):
                m = 4 * t + n
                pe.wait_ge(pqT_copied, m + 1)
                if m >= 1:
                    pe.wait_ge(keys_taken, m)
                for j in range(4):
                    mm = nc.tensor.matmul(Y[:, W + j * P:W + (j + 1) * P], pqT[:, n % 2, j, :], subk[:, 4 * n + j, :],
                                          start=True, stop=True)
                mm.then_inc(key_scores, 1)

            def slots(t, _):
                pe.wait_ge(route_ready, 4 * t + 4)
                for c, src in enumerate((sel[:, 0, :], sel[:, 1, :], gate[:, :])):
                    mm = nc.tensor.transpose(Y[:, c * P:(c + 1) * P], src, idm)
                mm.then_inc(slot_psum, 1)

            def gmap(t, span):
                for m in range(*span):
                    n = t * (P // G4) + m
                    pe.wait_ge(hot2_ready, n + 1)
                    pe.wait_ge(hot1_ready, n + 1)
                    if n >= 2:
                        pe.wait_ge(gmap_copied, n - 1)
                    for i in range(G4):
                        y0 = (n % 2) * W + i * P
                        mm = nc.tensor.matmul(Y[:, y0:y0 + P], onehot[:, n % HOTS, i, 1, :], onehot[:, n % HOTS, i, 0, :],
                                              start=True, stop=True)
                    mm.then_inc(gmap_psum, 1)

            def dense_u(b, j):
                pe.wait_ge(u_split, b * EB + (j + 1))
                if not (isinstance(b, int) and b == 0):
                    pe.wait_ge(act_ready, b * EB + (j + 1 - EB))
                for k in range(KD):
                    nc.tensor.matmul(bank(j), u_hi[:, j, k, :], h_hi[:, k, :], start=(k == 0), stop=False)
                    nc.tensor.matmul(bank(j), u_hi[:, j, k, :], h_lo[:, k, :], start=False, stop=False)
                    mm = nc.tensor.matmul(bank(j), u_lo[:, j, k, :], h_hi[:, k, :], start=False, stop=(k == KD - 1))
                mm.then_inc(pre_ready, 1)

            def dense_v(b, parity, h):
                pe.wait_ge(w_split, b * EB + EB)
                pe.wait_ge(v_split, b * 2 + (h + 1))
                for o in range(NT):
                    if h or not (isinstance(b, int) and b == 0):
                        pe.wait_ge(part_added, b * (2 * NT) + (NT * h + o + 1 - NT))
                    q = slice(o * P, (o + 1) * P)
                    for j in range(EB):
                        nc.tensor.matmul(part_bank(o), w_hi[parity][:, j, q], v_hi[h][:, j, :],
                                         start=(j == 0), stop=False)
                        nc.tensor.matmul(part_bank(o), w_hi[parity][:, j, q], v_lo[h][:, j, :],
                                         start=False, stop=False)
                        mm = nc.tensor.matmul(part_bank(o), w_lo[parity][:, j, q], v_hi[h][:, j, :], start=False, stop=(j == EB - 1))
                    mm.then_inc(part_ready, 1)

            def dense_block(b, parity):
                for h in range(2):
                    dense_u(b, 2 * h)
                    dense_u(b, 2 * h + 1)
                    dense_v(b - 1, (parity + 1) % 2, h)

            def dense(t, j):
                if j == 0:
                    pe.wait_ge(h_split, 1)
                dense_u(j // EB, j % EB)

            pe.wait_ge(early_in, 32)
            for i in range(2):
                pe.wait_ge(xn_ready, i + 1)
                turn(SC[:, i * D:(i + 1) * D], xn[i], tiles[token_order[i]][1]).then_inc(xT_ready, 1)
            pe.wait_ge(hT_ready, 2)

            def normT(t, i):
                pe.wait_ge(xn_ready, i + 1)
                pe.wait_ge(hT_ready, i)
                turn(Y, xn[i % 2]).then_inc(xT_ready, 1)

            work_of = {"kv": kv, "kT": kT_, "forget": forget, "q": q, "qT": qT_, "maps": maps, "unit": unit,
                       "heads_out": heads_out,
                       "gate": gate_, "yT": yT_, "branch": branch, "merge": merge, "out": out_, "h2T": h2T_,
                       "pq": pq_, "keys": keys, "slots": slots, "gmap": gmap, "dense": dense, "normT": normT}
            for k, t, a in pe_order:
                if k in work_of:
                    work_of[k](t, a)
            pe.wait_ge(gmap_copied, N_GROUPS)
            dense_v(0, 0, 0)
            dense_v(0, 0, 1)
            with pe.Fori(1, NB // 2) as c:
                dense_block(c * 2, 0)
                dense_block(c * 2 + 1, 1)
            dense_v(NB - 1, 1, 0)
            dense_v(NB - 1, 1, 1)

        @block.scalar
        def _(act):
            steps, roots = [0], [0]

            def after(ins):
                steps[0] += 1
                ins.then_inc(act_step, 1)
                act.wait_ge(act_step, steps[0])

            def squares(dst, src, acc=None):
                nc.scalar.activation(dst, src, ACT.Square, accum_out=acc).then_inc(sq_ready, 1)

            def root(r, n):
                roots[0] += 1
                act.wait_ge(var_ready, roots[0])
                nc.scalar.activation(std[0:r, 0:n], ss[0:r, 0:n], ACT.Sqrt).then_inc(std_ready, 1)

            def copy(dst, src, signal):
                nc.scalar.activation(dst, src, ACT.Copy).then_inc(signal, 1)

            def head_squares(key, src, r):
                if head_no[key] >= 1:
                    act.wait_ge(heads_ready, head_no[key])
                squares(qA[0:r, :], src[0:r, :])
                root(r, 8)

            def kv(t, a):
                p, g = a
                for i, s in enumerate(PASSES[p]):
                    r = tiles[s][1]
                    if g < 2 and i >= 2:
                        continue
                    wait_kv(act, p, g, i)
                    src = bank(kv_bank(p, g, i))
                    if g < 2:
                        head_squares(("k", p, g, i), src, r)
                    else:
                        copy(V[0:r, g - 2, s, :], src[0:r, :], v_copied)

            def kT_(t, a):
                p, g = a
                if len(PASSES[p]) > 2:
                    wait_kv(act, p, g, 2)
                    head_squares(("k", p, g, 2), bank(kv_bank(p, g, 2)), P)

            def forget(t, p):
                act.wait_ge(f_neg, p + 1)
                for s in PASSES[p]:
                    r = tiles[s][1]
                    ins = nc.scalar.activation(cum2[0:r, s, 0:8], cum2[0:r, s, 8:16], ACT.Exp)
                after(ins)
                for s in PASSES[p]:
                    r = tiles[s][1]
                    ins = nc.scalar.activation(cum2[0:r, s, 0:8], cum2[0:r, s, 0:8], ACT.Ln, bias=1.0)
                ins.then_inc(f_soft, 1)

            def q(t, g):
                act.wait_ge(chunk_done, group_done(KD, "q", t, g))
                head_squares(("q", t, g), bank(g), P)

            def exps(t, c):
                n = 16 * t + c
                act.wait_ge(max_ready, n + 1)
                if c >= 4:
                    v = c - 4
                    act.wait_ge(PT_ready, 12 * t + (v // 2 if v < 8 else v - 4) + 1)
                b, width = (c % 2) * 2 * W, (t + 1) * P + N_META
                nc.scalar.activation(probs[c % 4][:, 0:width], SC[:, b:b + width], ACT.Exp, bias=nmax[:, c:c + 1],
                                     accum_out=psum_p[:, c:c + 1]).then_inc(exp_ready, 1)

            def maps(t, u):
                if u < N_DIFF:
                    exps(t, 2 * u)
                    exps(t, 2 * u + 1)
                else:
                    if u == N_DIFF:
                        exps(t, u + N_DIFF)
                    if u + 1 < 12:
                        exps(t, u + 1 + N_DIFF)

            def unit(t, u):
                n = 12 * t + u
                act.wait_ge(PT_ready, n + 1)
                if n >= 2:
                    act.wait_ge(pv_done, n - 1)
                copy(PT[u % 2][:, 0:(t + 1) * P], TR[:, 0:(t + 1) * P], PT_copied)

            def heads_out(t, _):
                act.wait_ge(od_copied, t + 1)
                squares(ysq, ya)
                root(P, 4)

            def gate_(t, n):
                act.wait_ge(ya_ready, t + 1)
                act.wait_ge(chunk_done, group_done(KD, "gate", t, n))
                nc.scalar.activation(tg[:, n, :], bank(n), ACT.Tanh, scale=0.5).then_inc(tanh_ready, 1)

            def merge(t, _):
                act.wait_ge(mT_psum, t + 1)
                copy(mT.rearrange("p k q -> p (k q)"), SC[:, 0:D], mT_ready)

            def h2_(t, _):
                act.wait_ge(hs_ready, 2 * t + 2)
                squares(hsq, hs[:, t, :], ss[:, 0:1])
                root(P, 1)

            def pq_(t, n):
                m = 4 * t + n
                act.wait_ge(chunk_done, group_done(KD, "pq", t, n))
                if m >= 2:
                    act.wait_ge(key_scores, m - 1)
                copy(pqT[:, n % 2, :, :].rearrange("p j q -> p (j q)"), Y[:, 0:W], pqT_copied)

            def numbers(t, a):
                n, c = a
                m = 4 * t + n
                if c:
                    return
                act.wait_ge(gate_shift, m + 1)
                g_ = gate[:, n * 2 * TOPK:(n + 1) * 2 * TOPK]
                nc.scalar.activation(g_, g_, ACT.Exp).then_inc(gate_exp, 1)

            def gmap(t, span):
                for m in range(*span):
                    n = t * (P // G4) + m
                    blk, i = divmod(n, GT // G4)
                    act.wait_ge(gmap_psum, n + 1)
                    if i == 0 and blk >= 2:
                        act.wait_ge(gmap_stored[blk % 2], 16 * (blk // 2))
                    copy(gbuf[:, blk % 2, :, i * G4:(i + 1) * G4].rearrange("p e t -> p t e"),
                         Y[:, (n % 2) * W:(n % 2 + 1) * W].rearrange("p (t e) -> p t e", t=G4), gmap_copied)
                    if i == GT // G4 - 1:
                        act.wait_ge(gmap_copied, n + 1)
                        act.dma_start(gate_map[blk], gbuf[:, blk % 2, :, :]).then_inc(gmap_stored[blk % 2], 16)

            def high(dst, src, signal):
                nc.scalar.activation(dst, src, ACT.Copy).then_inc(signal, 1)

            def u_high_(b, j):
                act.wait_ge(u_landed[j], b * 16 + 16)
                high(u_hi[:, j, :, :], u_whole[:, j, :, :], u_high)

            def v_high_(b, h):
                act.wait_ge(v_landed[h], b * 16 + 16)
                high(v_hi[h], v_whole[h], v_high)

            def gelu(b, parity, j):
                act.wait_ge(pre_ready, b * EB + (j + 1))
                if j == 0 and not (isinstance(b, int) and b < 2):
                    act.wait_ge(part_ready, b * (2 * NT) - 2 * NT)
                nc.scalar.activation(w_whole[parity][:, j, :], bank(j), ACT.Gelu).then_inc(act_ready, 1)

            def w_high_(b, parity, j):
                act.wait_ge(w_gated, b * EB + (j + 1))
                high(w_hi[parity][:, j, :], w_whole[parity][:, j, :], w_high)

            def dense_block(b, parity, last=False):
                for j in range(EB):
                    if j < 2:
                        u_high_(b, j + 2)
                    elif not last:
                        u_high_(b + 1, j - 2)
                    if j % 2 == 0:
                        v_high_(b - 1, j // 2)
                    gelu(b, parity, j)
                    if j == 0:
                        w_high_(b - 1, (parity + 1) % 2, EB - 1)
                    else:
                        w_high_(b, parity, j - 1)

            def split(t, _):
                act.wait_ge(h2T_ready, NT)
                act.wait_ge(u_landed[0], 16)
                high(h_hi, h2T, h_high)
                u_high_(0, 0)
                u_high_(0, 1)

            def dense(t, j):
                u_high_((j + 2) // EB, (j + 2) % EB)
                gelu(j // EB, j // EB, j % EB)

            def norm(t, i):
                r = tiles[token_order[i]][1]
                act.wait_ge(x_in[i % 2], 16 * (i // 2 + 1))
                if i >= 1:
                    act.wait_ge(xn_ready, i)
                    act.wait_ge(std_ready, roots[0])
                squares(xsq[0:r, :], xin[i % 2][0:r, :], ss[0:r, 0:1])
                root(r, 1)

            norm(0, 0)
            norm(0, 1)
            act.wait_ge(lam_dots, 2)
            nc.scalar.activation(lamt[:, 2:4], lamt[:, 0:2], ACT.Exp).then_inc(lam_exp, 1)
            work_of = {"kv": kv, "kT": kT_, "forget": forget, "q": q, "maps": maps, "unit": unit,
                       "heads_out": heads_out, "gate": gate_,
                       "merge": merge, "h2": h2_, "pq": pq_, "numbers": numbers,
                       "gmap": gmap, "split": split, "dense": dense, "norm": norm}
            for k, t, a in order:
                if k in work_of:
                    work_of[k](t, a)
            v_high_(0, 0)
            for j in range(EB):
                w_high_(0, 0, j)
            v_high_(0, 1)
            for j in range(EB - 1):
                w_high_(1, 1, j)
            with act.Fori(1, NB // 2 - 1) as c:
                dense_block(c * 2, 0)
                dense_block(c * 2 + 1, 1)
            dense_block(NB - 2, 0)
            dense_block(NB - 1, 1, last=True)
            w_high_(NB - 1, 1, EB - 1)
            v_high_(NB - 1, 0)
            v_high_(NB - 1, 1)

        @block.vector
        def _(dve):
            steps, sums = [0], [0]

            def after(ins):
                steps[0] += 1
                ins.then_inc(dve_step, 1)
                dve.wait_ge(dve_step, steps[0])

            def wait_squares():
                sums[0] += 1
                dve.wait_ge(sq_ready, sums[0])

            def inverse_root(r, n, width, scale=None):
                nc.vector.tensor_scalar(ss[0:r, 0:n], ss[0:r, 0:n], 1.0 / width, EPS, ALU.mult,
                                        ALU.add).then_inc(var_ready, 1)
                dve.wait_ge(std_ready, sums[0])
                after(nc.vector.reciprocal(rstd[0:r, 0:n], std[0:r, 0:n]))
                if scale is not None:
                    after(nc.vector.tensor_scalar(rstd[0:r, 0:n], rstd[0:r, 0:n], scale, None, ALU.mult))

            v3 = lambda a: a.rearrange("p (g d) -> p g d", g=8)

            def norm_heads(key, r, psum, which, tile, scale):
                i = head_no[key]
                wait_squares()
                after(nc.vector.tensor_reduce(ss[0:r, 0:8], v3(qA[0:r, :]), AX.X, ALU.add))
                inverse_root(r, 8, DH, scale)
                rb = rstd[0:r, 0:8].unsqueeze(2).to_broadcast([r, 8, DH])
                hd = heads[i % 2]
                if i >= 2:
                    dve.wait_ge(headsT_ready, i - 1)
                if which is None:
                    nc.vector.tensor_tensor(v3(hd[0:r, :]), v3(psum[0:r, :]), rb, ALU.mult).then_inc(heads_ready, 1)
                    return
                after(nc.vector.tensor_tensor(v3(qraw[0:r, :]), v3(psum[0:r, :]), rb, ALU.mult))
                C = ropeC[0:r, which, tile, :].unsqueeze(1).to_broadcast([r, 8, DH])
                S = ropeS[0:r, which, tile, :]
                nc.vector.tensor_tensor(v3(hd[0:r, :]), v3(qraw[0:r, :]), C, ALU.mult)
                H = DH // 2
                for lo, src in ((0, H), (H, 0)):
                    ins = nc.vector.tensor_tensor(v3(qA[0:r, :])[:, :, lo:lo + H], v3(qraw[0:r, :])[:, :, src:src + H],
                                                  S[:, lo:lo + H].unsqueeze(1).to_broadcast([r, 8, H]), ALU.mult)
                after(ins)
                nc.vector.tensor_tensor(hd[0:r, :], hd[0:r, :], qA[0:r, :], ALU.add).then_inc(heads_ready, 1)

            def put_T(key, dst, r, gain):
                dve.wait_ge(headsT_ready, head_no[key] + 1)
                src = TR[:, :].rearrange("p (j q) -> p j q", j=DPAIRS)[:, :, 0:r]
                if gain is None:
                    nc.vector.tensor_copy(dst, src).then_inc(qk_ready, 1)
                else:
                    nc.vector.tensor_scalar(dst, src, gain, None, ALU.mult).then_inc(qk_ready, 1)

            def kv(t, a):
                p, g = a
                if g < 2:
                    for i, s in enumerate(PASSES[p]):
                        if i >= 2:
                            continue
                        norm_heads(("k", p, g, i), tiles[s][1], bank(kv_bank(p, g, i)), 1 if g == 0 else None, s, None)

            def kT_(t, a):
                p, g = a
                for i, s in enumerate(PASSES[p]):
                    c0, r = tiles[s]
                    put_T(("k", p, g, i), kT[:, g, :, c0:c0 + r], r, None if g == 0 else small[:, K_FKG:K_FKG + 1])
                    if i == 0 and len(PASSES[p]) > 2:
                        s2 = PASSES[p][2]
                        norm_heads(("k", p, g, 2), P, bank(kv_bank(p, g, 2)), 1 if g == 0 else None, s2, None)

            def forget(t, p):
                dve.wait_ge(f_ready, p + 1)
                for s in PASSES[p]:
                    r = tiles[s][1]
                    z = TR[0:r, s * N_FOX:(s + 1) * N_FOX]
                    nc.vector.tensor_scalar(logf[0:r, s, :], z, 0.0, None, ALU.min)
                    after(nc.vector.tensor_scalar(cum2[0:r, s, 8:16], z, 0.0, None, ALU.max))
                    ins = nc.vector.tensor_tensor(cum2[0:r, s, 8:16], logf[0:r, s, :], cum2[0:r, s, 8:16],
                                                  ALU.subtract)
                ins.then_inc(f_neg, 1)
                dve.wait_ge(f_soft, p + 1)
                for s in PASSES[p]:
                    r = tiles[s][1]
                    ins = nc.vector.tensor_tensor(logf[0:r, s, :], logf[0:r, s, :], cum2[0:r, s, 0:8], ALU.subtract)
                ins.then_inc(logf_ready, 1)
                dve.wait_ge(cum_ready, p + 1)
                for s in PASSES[p]:
                    r = tiles[s][1]
                    for j in range(2):
                        ins = nc.vector.tensor_copy(cum2[0:r, s, 8 * j:8 * j + 8], TR[0:r, s * N_FOX:(s + 1) * N_FOX])
                ins.then_inc(cum_copied, 1)
                dve.wait_ge(cumT_ready, p + 1)
                for i, s in enumerate(PASSES[p]):
                    c0, r = tiles[s]
                    src = TR[0:16, i * P:i * P + r]
                    ins = nc.vector.tensor_scalar(decR[:, c0:c0 + r], src, small[0:16, K_ROW0:K_ROW0 + 1],
                                                  small[0:16, K_ROW1:K_ROW1 + 1], ALU.mult, ALU.add)
                    if s < NT:
                        ins = nc.vector.tensor_copy(cumT[:, c0:c0 + r], src)
                ins.then_inc(dec_ready, 1)

            def q(t, g):
                norm_heads(("q", t, g), P, bank(g), 0 if g == 0 else None, t, DH ** -0.5)

            def qT_(t, g):
                put_T(("q", t, g), qT[g], P, None if g == 0 else small[:, K_FQG:K_FQG + 1])
                if g == 1:
                    dve.wait_ge(dec_ready, t + (2 if t else 1))
                    for h in range(N_FOX):
                        ins = nc.vector.tensor_scalar(decL[h // 4][:, h % 4, :], cumT[:, t * P:(t + 1) * P],
                                                      small[0:16, K_LSEL + h:K_LSEL + h + 1],
                                                      small[0:16, K_LNEG + h:K_LNEG + h + 1], ALU.mult, ALU.add)
                    ins.then_inc(dec_ready, 1)

            def row_max(t, c):
                dve.wait_ge(scores_ready, 16 * t + c + 1)
                b = (c % 2) * 2 * W
                nc.vector.tensor_reduce(nmax[:, c:c + 1], SC[:, b:b + (t + 1) * P + N_META], AX.X, ALU.max,
                                        negate=True).then_inc(max_ready, 1)

            def maps(t, u):
                if u < N_DIFF:
                    row_max(t, 2 * u)
                    row_max(t, 2 * u + 1)
                else:
                    if u == N_DIFF:
                        row_max(t, u + N_DIFF)
                    if u + 1 < 12:
                        row_max(t, u + 1 + N_DIFF)

            def unit(t, u):
                width = (t + 1) * P + N_META
                if u < N_DIFF:
                    c = 2 * u
                    p0, p1 = probs[c % 4][:, 0:width], probs[c % 4 + 1][:, 0:width]
                    dve.wait_ge(exp_ready, 16 * t + c + 2)
                    after(nc.vector.reciprocal(rsum[:, c:c + 2], psum_p[:, c:c + 2]))
                    nc.vector.tensor_scalar(p0, p0, rsum[:, c:c + 1], None, ALU.mult)
                    after(nc.vector.tensor_scalar(rsum[:, c + 1:c + 2], rsum[:, c + 1:c + 2], lamt[:, 5:6], None,
                                                  ALU.mult))
                    nc.vector.scalar_tensor_tensor(out=p1, in0=p1, scalar=rsum[:, c + 1:c + 2], in1=p0,
                                                   op0=ALU.mult, op1=ALU.add).then_inc(mix_ready, 1)
                n = 12 * t + u
                dve.wait_ge(PT_ready, n + 1)
                if n >= 2:
                    dve.wait_ge(pv_done, n - 1)
                nc.vector.tensor_copy(PT[u % 2][0:N_META, SEQ:SEQ + P],
                                      meta_T(2 * u + 1 if u < N_DIFF else u + N_DIFF)).then_inc(PTm_copied, 1)
                if u == N_DIFF:
                    dve.wait_ge(pv_done, 12 * t + N_DIFF)
                    nc.vector.tensor_copy(ya, OV[:, :]).then_inc(od_copied, 1)

            def heads_out(t, _):
                after(nc.vector.reciprocal(rsum[:, 8:16], psum_p[:, 8:16]))
                dve.wait_ge(pv_done, 12 * (t + 1))
                nc.vector.tensor_tensor(v3(yb), v3(OV[:, :]), rsum[:, 8:16].unsqueeze(2).to_broadcast([P, 8, DH]),
                                        ALU.mult).then_inc(yb_ready, 1)
                wait_squares()
                after(nc.vector.tensor_reduce(ss[:, 0:4], ysq.rearrange("p (h d) -> p h d", h=4), AX.X, ALU.add))
                inverse_root(P, 4, DV)
                y3 = ya.rearrange("p (h d) -> p h d", h=4)
                nc.vector.tensor_tensor(y3, y3, rstd[:, 0:4].unsqueeze(2).to_broadcast([P, 4, DV]),
                                        ALU.mult).then_inc(ya_ready, 1)

            def yT_(t, b):
                dve.wait_ge(yT_psum, 2 * t + b + 1)
                dst = yT[:, b, :, :].rearrange("p k q -> p (k q)")
                if b == 0:
                    nc.vector.tensor_scalar(dst, TR[:, :], small[:, K_SUB:K_SUB + 1], 1.0 - LAMBDA_INIT,
                                            ALU.mult, ALU.mult).then_inc(yT_ready, 1)
                else:
                    nc.vector.tensor_copy(dst, TR[:, :]).then_inc(yT_ready, 1)

            def merge(t, _):
                for n in range(2):
                    dve.wait_ge(chunk_done, group_done(4, "branch", t, 2 + n))
                    nc.vector.scalar_tensor_tensor(out=tg[:, n, :], in0=tg[:, n, :], scalar=1.0, in1=bank(n),
                                                   op0=ALU.add, op1=ALU.mult)
                    after(nc.vector.scalar_tensor_tensor(out=tg[:, 2 + n, :], in0=tg[:, 2 + n, :], scalar=1.0,
                                                         in1=bank(2 + n), op0=ALU.add, op1=ALU.mult))
                    nc.vector.tensor_tensor(merged[:, n * W:(n + 1) * W], tg[:, n, :], tg[:, 2 + n, :],
                                            ALU.add).then_inc(merged_ready, 1)

            def out_(t, n):
                dve.wait_ge(chunk_done, group_done(KD, "out", t, n))
                if n == 0 and t == 0:
                    dve.wait_ge(res_in, 16 * NT)
                hb = hs[:, t, n * W:(n + 1) * W]
                nc.vector.scalar_tensor_tensor(out=hb, in0=bank(2 + n), scalar=0.5, in1=hb, op0=ALU.mult,
                                               op1=ALU.add).then_inc(hs_ready, 1)

            def h2_(t, _):
                wait_squares()
                inverse_root(P, 1, D)
                nc.vector.tensor_scalar(h2, hs[:, t, :], rstd[:, 0:1], None, ALU.mult).then_inc(h2_ready, 1)

            def h2T_(t, _):
                dve.wait_ge(h2T_psum, t + 1)
                nc.vector.tensor_tensor(h2T[:, :, t * P:(t + 1) * P], SC[:, 0:D].rearrange("p (k q) -> p k q", k=KD),
                                        small[:, K_FFNG:K_FFNG + KD].unsqueeze(2).to_broadcast([P, KD, P]),
                                        ALU.mult).then_inc(h2T_ready, 1)

            def top16(vals, inds, src, n, signal=None, value=None):
                after(nc.vector.max(vals[:, 0:8], src))
                nc.vector.max_index(inds[:, 0:8], vals[:, 0:8], src)
                ins = nc.vector.match_replace(scrap[:, 0:n], vals[:, 0:8], src, LOWEST)
                if signal is not None:
                    ins.then_inc(signal, 1)
                    dve.wait_ge(signal, value)
                else:
                    after(ins)
                after(nc.vector.max(vals[:, 8:16], scrap[:, 0:n]))
                after(nc.vector.max_index(inds[:, 8:16], vals[:, 8:16], scrap[:, 0:n]))

            def keys(t, n):
                dve.wait_ge(key_scores, 4 * t + n + 1)
                top_keys(t, (n, 0))

            def top_keys(t, a):
                n, j = a
                top16(top[:, 4 * n + j, :], topi[:, 4 * n + j, :], Y[:, W + j * P:W + (j + 1) * P], NKEYS,
                      keys_taken if j == 3 else None, 4 * t + n + 1)

            def pairs(t, a):
                n, i = a
                h = 2 * n + i
                after(nc.vector.tensor_tensor(cand.rearrange("p (a b) -> p a b", a=TOPK),
                                              top[:, 2 * h, :].unsqueeze(2).to_broadcast([P, TOPK, TOPK]),
                                              top[:, 2 * h + 1, :].unsqueeze(1).to_broadcast([P, TOPK, TOPK]),
                                              ALU.add))
                top16(best[:, h, :], posn[:, h, :], cand, TOPK * TOPK)
                if i == 0:
                    return
                hh, e0 = slice(2 * n, 2 * n + 2), n * 2 * TOPK
                if t >= 1 and n == 0:
                    dve.wait_ge(slot_psum, t)
                g2 = gate[:, e0:e0 + 2 * TOPK].rearrange("p (h k) -> p h k", h=2)
                nc.vector.tensor_tensor(g2, best[:, hh, :], best[:, hh, 0:1].to_broadcast([P, 2, TOPK]),
                                        ALU.subtract).then_inc(gate_shift, 1)
                nc.vector.tensor_copy(topf[:, 4 * n:4 * n + 4, :], topi[:, 4 * n:4 * n + 4, :])
                nc.vector.tensor_scalar(posa[:, 0, :, :], posn[:, hh, :], 4, None, ALU.logical_shift_right)
                after(nc.vector.tensor_scalar(posa[:, 1, :, :], posn[:, hh, :], TOPK - 1, None, ALU.bitwise_and))
                after(nc.vector.tensor_copy(choice[:, 1856:1920], choice[:, 1792:1856].bitcast(U32)))

            def numbers(t, a):
                n, c = a
                m = 4 * t + n
                hh, e0 = slice(2 * n, 2 * n + 2), n * 2 * TOPK
                g2 = gate[:, e0:e0 + 2 * TOPK].rearrange("p (h k) -> p h k", h=2)
                if m == 0 and c == 0:
                    dve.wait_ge(iota_ready, 2)
                for h in range(2):
                    ins = nc.vector.tensor_tensor(hot[:, h, :, :],
                                                  posf[:, c, h, :].unsqueeze(2).to_broadcast([P, TOPK, TOPK]),
                                                  iota16[:, :].unsqueeze(1).to_broadcast([P, TOPK, TOPK]),
                                                  ALU.is_equal)
                after(ins)
                for h in range(2):
                    ins = nc.vector.tensor_tensor(hot[:, h, :, :], hot[:, h, :, :],
                                                  topf[:, 4 * n + 2 * h + c, :].unsqueeze(1)
                                                  .to_broadcast([P, TOPK, TOPK]), ALU.mult)
                after(ins)
                after(nc.vector.tensor_reduce(sel[:, c, e0:e0 + 2 * TOPK],
                                              hot.rearrange("p h k a -> p (h k) a"), AX.X, ALU.add))
                if c == 0:
                    return
                dve.wait_ge(gate_exp, m + 1)
                after(nc.vector.tensor_reduce(gsum[:, 0, hh], g2, AX.X, ALU.add))
                after(nc.vector.reciprocal(gsum[:, 1, hh], gsum[:, 0, hh]))
                nc.vector.tensor_tensor(g2, g2, gsum[:, 1, hh].unsqueeze(2).to_broadcast([P, 2, TOPK]),
                                        ALU.mult).then_inc(route_ready, 1)

            def slots(t, _):
                dve.wait_ge(slot_psum, t + 1)
                if t:
                    dve.wait_ge(hot2_ready, t * (P // G4))
                nc.vector.tensor_copy(slot[:, :, :].rearrange("p c q -> p (c q)"), Y[:, 0:3 * P]).then_inc(slot_ready, 1)
                dve.wait_ge(slot_ready, t + 1)

            def gmap(t, span):
                m0, m1 = (m + AHEAD if m else 0 for m in span)
                for m in range(m0, min(m1, P // G4)):
                    n = t * (P // G4) + m
                    if n >= HOTS:
                        dve.wait_ge(gmap_psum, n - HOTS + 1)
                    for i in range(G4):
                        q_ = m * G4 + i
                        ins = nc.vector.tensor_scalar(onehot[:, n % HOTS, i, 0, :], iota128[:, :],
                                                      slot[:, 0, q_:q_ + 1], slot[:, 2, q_:q_ + 1],
                                                      ALU.is_equal, ALU.mult)
                    ins = nc.vector.tensor_tensor(onehot[:, n % HOTS, POOLS:G4, 1, :],
                                                  iota128[:, :].unsqueeze(1).to_broadcast([P, G4 - POOLS, NKEYS]),
                                                  slot[:, 1, m * G4 + POOLS:(m + 1) * G4].unsqueeze(2)
                                                  .to_broadcast([P, G4 - POOLS, NKEYS]), ALU.is_equal)
                    ins.then_inc(hot1_ready, 1)

            def low(lo, whole, hi, signal):
                nc.vector.tensor_tensor(lo, whole, hi.bitcast(F32), ALU.subtract).then_inc(signal, 1)

            def u_low(b, j):
                if isinstance(b, int) and b * EB + j == EARLY:
                    dve.wait_ge(u_split, EARLY)
                dve.wait_ge(u_high, b * EB + (j + 1))
                low(u_lo[:, j, :, :], u_whole[:, j, :, :], u_hi[:, j, :, :], u_split)

            def v_low(b, h):
                dve.wait_ge(v_high, b * 2 + (h + 1))
                low(v_lo[h], v_whole[h], v_hi[h], v_split)

            def times_gate(b, parity, j, g_loads):
                if j == 0:
                    dve.wait_ge(g_landed[parity], g_loads * 16)
                dve.wait_ge(act_ready, b * EB + (j + 1))
                w3 = w_whole[parity][:, j, :].rearrange("p (b t) -> p b t", b=GBLK)
                nc.vector.tensor_tensor(w3, w3, gates[parity][:, :, j, :], ALU.mult).then_inc(w_gated, 1)

            def w_low(b, parity, j):
                dve.wait_ge(w_high, b * EB + (j + 1))
                low(w_lo[parity][:, j, :], w_whole[parity][:, j, :], w_hi[parity][:, j, :], w_split)

            def add_parts(b, h):
                for o in range(NT):
                    dve.wait_ge(part_ready, b * (2 * NT) + (NT * h + o + 1))
                    if not (isinstance(b, int) and b == 0):
                        dve.wait_ge(part_added, b * (2 * NT) + (NT * h + o + 1 - 2 * NT))
                    y = hs[:, o, h * W:(h + 1) * W]
                    nc.vector.tensor_tensor(y, y, part_bank(o), ALU.add).then_inc(part_added, 1)

            def dense_block(b, parity, g_loads, last=False):
                for j in range(EB):
                    if j < 2:
                        u_low(b, j + 2)
                    elif not last:
                        u_low(b + 1, j - 2)
                    if j % 2 == 0:
                        v_low(b - 1, j // 2)
                    times_gate(b, parity, j, g_loads)
                    if j == 0:
                        w_low(b - 1, (parity + 1) % 2, EB - 1)
                    else:
                        w_low(b, parity, j - 1)
                    if j % 2:
                        add_parts(b - 1, j // 2)

            def split(t, _):
                dve.wait_ge(h_high, 1)
                low(h_lo, h2T, h_hi, h_split)

            def dense(t, j):
                if j + 2 >= EARLY:
                    u_low((j + 2) // EB, (j + 2) % EB)

            nc.vector.memset(ones[:, :], 1.0)
            nc.vector.memset(cum2[:, :, :], 0.0)
            after(nc.vector.memset(logf[:, :, :], 0.0))
            def norm(t, i):
                r = tiles[token_order[i]][1]
                wait_squares()
                inverse_root(r, 1, D)
                if i >= 2:
                    dve.wait_ge(xT_ready, i - 1)
                nc.vector.tensor_scalar(xn[i % 2][0:r, :], xin[i % 2][0:r, :], rstd[0:r, 0:1], None,
                                        ALU.mult).then_inc(xn_ready, 1)

            def normT(t, i):
                c0, r = tiles[token_order[i]]
                dve.wait_ge(xT_ready, i + 1)
                src = SC[:, i * D:(i + 1) * D] if i < 2 else Y[:, :]
                nc.vector.tensor_tensor(hT[:, :, c0:c0 + r], src.rearrange("p (k q) -> p k q", k=KD)[:, :, 0:r],
                                        small[:, K_MIXG:K_MIXG + KD].unsqueeze(2).to_broadcast([P, KD, r]),
                                        ALU.mult).then_inc(hT_ready, 1)

            norm(0, 0)
            norm(0, 1)
            normT(0, 0)
            normT(0, 1)

            dve.wait_ge(consts_in, CONSTS)
            nc.vector.tensor_copy(mask_bf[:, :, :].rearrange("p b k -> p (b k)"), work[:, 2048:2048 + 2 * P])
            after(nc.vector.tensor_copy(ident_bf[:, :], ident[:, 0:P]))
            rw = work[:, 4096:4096 + R_W]
            qg, kg, lam = rw[:, 0:DH], rw[:, DH:2 * DH], rw[:, 2 * DH:2 * DH + 4 * DH]
            H = DH // 2
            for which, g in ((1, kg), (0, qg)):
                def gb(lo, hi):
                    return g[:, lo:hi].unsqueeze(1).to_broadcast([P, NKT, hi - lo])
                nc.vector.tensor_tensor(ropeC[:, which, :, :], ropeC[:, 0, :, :], gb(0, DH), ALU.mult)
                nc.vector.tensor_tensor(ropeS[:, which, :, 0:H], ropeS[:, 0, :, 0:H], gb(H, DH), ALU.mult)
                after(nc.vector.tensor_tensor(ropeS[:, which, :, H:DH], ropeS[:, 0, :, H:DH], gb(0, H), ALU.mult))
            for i in range(2):
                nc.vector.tensor_tensor_reduce(out=work[:, 5120:5120 + DH], in0=lam[:, 2 * i * DH:(2 * i + 1) * DH],
                                               in1=lam[:, (2 * i + 1) * DH:(2 * i + 2) * DH], scale=1.0, scalar=0.0,
                                               op0=ALU.mult, op1=ALU.add,
                                               accum_out=lamt[:, i:i + 1]).then_inc(lam_dots, 1)
                dve.wait_ge(lam_dots, i + 1)
            dve.wait_ge(lam_exp, 1)
            after(nc.vector.tensor_tensor(lamt[:, 4:5], lamt[:, 3:4], lamt[:, 2:3], ALU.subtract))
            nc.vector.tensor_scalar(lamt[:, 5:6], lamt[:, 4:5], -LAMBDA_INIT, None, ALU.add).then_inc(setup, 1)
            dve.wait_ge(setup, 1)

            work_of = {"kv": kv, "kT": kT_, "forget": forget, "q": q, "qT": qT_, "maps": maps, "unit": unit,
                       "heads_out": heads_out,
                       "yT": yT_, "merge": merge, "out": out_, "h2": h2_, "h2T": h2T_, "keys": keys, "top": top_keys,
                       "pairs": pairs, "numbers": numbers, "slots": slots, "gmap": gmap, "split": split, "dense": dense,
                       "norm": norm, "normT": normT}
            for k, t, a in order:
                if k in work_of:
                    work_of[k](t, a)
            v_low(0, 0)
            for j in range(EB):
                times_gate(0, 0, j, 1)
                if j:
                    w_low(0, 0, j - 1)
            w_low(0, 0, EB - 1)
            v_low(0, 1)
            for j in range(EB):
                times_gate(1, 1, j, 1)
                if j:
                    w_low(1, 1, j - 1)
            add_parts(0, 0)
            add_parts(0, 1)
            with dve.Fori(1, NB // 2 - 1) as c:
                dense_block(c * 2, 0, c + 1)
                dense_block(c * 2 + 1, 1, c + 1)
            dense_block(NB - 2, 0, NB // 2)
            dense_block(NB - 1, 1, NB // 2, last=True)
            w_low(NB - 1, 1, EB - 1)
            for h in range(2):
                v_low(NB - 1, h)
                add_parts(NB - 1, h)

        @block.gpsimd
        def _(pool):
            nc.gpsimd.iota(iota16[:, :], pattern=[[1, TOPK]], base=0, channel_multiplier=0,
                           allow_small_or_imprecise_dtypes=True).then_inc(iota_ready, 1)
            nc.gpsimd.iota(iota128[:, :], pattern=[[1, NKEYS]], base=0, channel_multiplier=0,
                           allow_small_or_imprecise_dtypes=True).then_inc(iota_ready, 1)
            pool.wait_ge(iota_ready, 2)

            def u_low(n):
                pool.wait_ge(u_high, n + 1)
                j = n % EB
                nc.gpsimd.tensor_tensor(u_lo[:, j, :, :], u_whole[:, j, :, :], u_hi[:, j, :, :].bitcast(F32),
                                        ALU.subtract).then_inc(u_split, 1)

            for t in range(NT):
                if t == NT - 1:
                    for n in range(EARLY):
                        u_low(n)
                pool.wait_ge(slot_ready, t + 1)
                for m in range(P // G4):
                    n = t * (P // G4) + m
                    if n >= HOTS:
                        pool.wait_ge(gmap_psum, n - HOTS + 1)
                    for i in range(POOLS):
                        q_ = m * G4 + i
                        ins = nc.gpsimd.tensor_scalar(onehot[:, n % HOTS, i, 1, :], iota128[:, :],
                                                      slot[:, 1, q_:q_ + 1], None, ALU.is_equal)
                    ins.then_inc(hot2_ready, 1)


def kernel(**inputs):
    import numpy as np
    import concourse.bacc as bacc
    from concourse.bass_utils import run_bass_kernel_spmd

    nc = bacc.Bacc("TRN2", target_bir_lowering=False, num_devices=1)

    def flat(name):
        return np.ascontiguousarray(np.asarray(inputs[name])[0])

    tri = (np.arange(P)[:, None] <= np.arange(P)[None, :]).astype(np.float32)
    col = np.arange(P)[None, :]
    row = np.arange(P)[:, None]
    mask_f = np.where(col <= row, 0.0, MASKED)
    mask_d = np.where(col // CHUNK <= row // CHUNK, 0.0, MASKED)
    table = np.concatenate([np.eye(P), tri, mask_d, mask_f], axis=1).astype(np.float32)
    pos = np.concatenate([np.arange(SEQ) + N_META, np.arange(N_META), np.zeros(P - N_META)]).astype(np.float32)
    inv = np.float32(ROPE_THETA) ** (-np.arange(0, DH, 2, dtype=np.float32) / np.float32(DH))
    ang = pos[:, None] * inv[None, :].astype(np.float32)
    cos, sin = np.cos(ang), np.sin(ang)
    rope = np.concatenate([cos, cos, -sin, sin], axis=1).astype(np.float32)
    rope = np.ascontiguousarray(rope.reshape(NT + 1, P, 2 * DH).transpose(1, 0, 2))
    r = np.arange(P)
    lower = ((r >= 8) & (r < 16)).astype(np.float32)
    head = np.arange(N_FOX)[None, :]
    lsel = (r[:, None] == head).astype(np.float32)
    lneg = -(r[:, None] - 8 == head).astype(np.float32)

    two = lambda a: np.concatenate([a, a])[:, None]
    cols = np.concatenate([flat("norm_mix_g").reshape(KD, P).T, two(flat("fox_qnorm_g")), two(flat("fox_knorm_g")),
                           flat("diff_subln_g")[:, None], lower[:, None], 1.0 - lower[:, None], lsel, lneg,
                           flat("norm_ffn_g").reshape(KD, P).T], axis=1).astype(np.float32)
    rows = np.concatenate([flat("diff_qnorm_g"), flat("diff_knorm_g"),
                           flat("diff_lambda").reshape(-1)])
    arrays = {
        "x": np.ascontiguousarray(np.asarray(inputs["x"])[0]),
        "meta": np.ascontiguousarray(inputs["meta_tokens"]),
        "w_in": flat("w_in"), "b_gate": np.ascontiguousarray(inputs["b_gate"]),
        "b_forget": np.ascontiguousarray(inputs["b_forget"]),
        "w_bd": flat("w_branch_diff"), "w_bf": flat("w_branch_fox"), "w_out": flat("w_out"),
        "w_pq": flat("peer_w_q"),
        "subkeys_t": np.ascontiguousarray(flat("peer_subkeys").transpose(3, 0, 1, 2).reshape(P, 2 * PH, NKEYS)),
        "u_t": np.ascontiguousarray(flat("peer_u").reshape(NKEYS, NKEYS, KD, P).transpose(0, 3, 2, 1)),
        "v": flat("peer_v"),
        "table": table, "cols": cols, "rows": np.tile(rows[None, :], (P, 1)), "rope": rope,
    }
    aps = {n: nc.dram_tensor(n, a.shape, mybir.dt.from_np(a.dtype), kind="ExternalInput").ap()
           for n, a in arrays.items()}
    aps["gate_map"] = nc.dram_tensor("gate_map", (GBLK, P, NKEYS, GT), F32, kind="Internal").ap()
    out = nc.dram_tensor("out", (SEQ, D), F32, kind="ExternalOutput").ap()
    build(nc, **aps, out=out)
    res = run_bass_kernel_spmd(nc, [arrays], core_ids=[0])
    return res.results[0]["out"].reshape(1, SEQ, D)
```
